# Optimizing a Trainium2 kernel written in Bass

```python
import math
import jax
import jax.numpy as jnp
from jax import lax
import numpy as np

D_MODEL = 1024
BATCH = 1
SEQ = 2048
DEPTH = 1

GRID_W = 64
D_MIX = 1024
EPS = 1e-6

HG_HEADS = 4
HG_DK = 128
HG_DV = 128
HG_KW = HG_HEADS * HG_DK
HG_VW = HG_HEADS * HG_DV
CHUNK = 64

ATT_HEADS = 8
ATT_KV_HEADS = 2
ATT_DH = 64
ATT_GROUP = ATT_HEADS // ATT_KV_HEADS
ATT_QW = ATT_HEADS * ATT_DH
ATT_KVW = ATT_KV_HEADS * ATT_DH
ROPE_THETA = 10000.0
Q_BLOCK = 128

D_IN = 2 * HG_KW + HG_KW + 2 * HG_VW + ATT_QW + 2 * ATT_KVW

D_FF = -(-8 * D_MODEL // (3 * 256)) * 256

kernel_name = "hybrid_hgrn2_axial_gqa_encoder"

def _rmsnorm(x, w):
    xf = x.astype(jnp.float32)
    y = xf * lax.rsqrt(jnp.mean(xf * xf, axis=-1, keepdims=True) + EPS)
    return (y * w.astype(jnp.float32)).astype(x.dtype)

def _gla_chunk_scan(q, k, v, log_f):
    B, L, H, DK = q.shape
    DV = v.shape[-1]
    n = L // CHUNK

    def to_chunks(a):
        return a.reshape(B, n, CHUNK, H, a.shape[-1]).transpose(1, 0, 3, 2, 4)

    qc, kc, vc, gc = to_chunks(q), to_chunks(k), to_chunks(v), to_chunks(log_f)
    b = jnp.cumsum(gc, axis=3)
    b_ref = b[:, :, :, CHUNK // 2 - 1:CHUNK // 2, :]
    b_last = b[:, :, :, -1:, :]
    q_in = qc * jnp.exp(b - b_ref)
    k_in = kc * jnp.exp(b_ref - b)
    scores = jnp.einsum('nbhtk,nbhsk->nbhts', q_in, k_in)
    causal_in_scan = jnp.tril(jnp.ones((CHUNK, CHUNK), dtype=bool))
    scores = jnp.where(causal_in_scan, scores, 0.0)
    o_intra = jnp.einsum('nbhts,nbhsv->nbhtv', scores, vc)
    contrib = jnp.einsum('nbhsk,nbhsv->nbhkv', kc * jnp.exp(b_last - b), vc).astype(jnp.float32)
    decay = jnp.exp(b_last[:, :, :, 0, :]).astype(jnp.float32)

    def step(S, inp):
        d, c = inp
        return d[..., None] * S + c, S

    S0 = jnp.zeros((B, H, DK, DV), jnp.float32)
    _, S_prev = lax.scan(step, S0, (decay, contrib))
    o_inter = jnp.einsum('nbhtk,nbhkv->nbhtv', qc * jnp.exp(b), S_prev)
    o = (o_intra + o_inter).transpose(1, 0, 3, 2, 4).reshape(B, L, H, DV)
    return o.astype(v.dtype)

def _hgrn2_group(u_q, u_ff, u_fb, u_i, u_g, lb_fwd, lb_bwd, norm_w):
    B, L, _ = u_q.shape
    q = jax.nn.silu(u_q).reshape(B, L, HG_HEADS, HG_DK)
    i = u_i.reshape(B, L, HG_HEADS, HG_DV)

    def gates(z, lb):
        zf = z.astype(jnp.float32)
        f = lb + (1.0 - lb) * jax.nn.sigmoid(zf)
        k = (1.0 - lb) * jax.nn.sigmoid(-zf)
        return (jnp.log(f).reshape(B, L, HG_HEADS, HG_DK),
                k.reshape(B, L, HG_HEADS, HG_DK).astype(z.dtype))

    logf_f, k_f = gates(u_ff, lb_fwd)
    logf_b, k_b = gates(u_fb, lb_bwd)
    o_fwd = _gla_chunk_scan(q, k_f, i, logf_f)
    flip = lambda a: jnp.flip(a, axis=1)
    o_bwd = flip(_gla_chunk_scan(flip(q), flip(k_b), flip(i), flip(logf_b)))
    o = _rmsnorm(o_fwd + o_bwd, norm_w)
    o = o * jax.nn.silu(u_g.reshape(B, L, HG_HEADS, HG_DV))
    return o.reshape(B, L, HG_VW)

def _axial_rope_tables(L):
    rows = L // GRID_W
    row = jnp.repeat(jnp.arange(rows), GRID_W).astype(jnp.float32)
    col = jnp.tile(jnp.arange(GRID_W), rows).astype(jnp.float32)
    axis_dim = ATT_DH // 2
    freqs = ROPE_THETA ** (-jnp.arange(0, axis_dim, 2, dtype=jnp.float32) / axis_dim)
    ang = jnp.concatenate([row[:, None] * freqs, col[:, None] * freqs], axis=-1)
    return jnp.cos(ang), jnp.sin(ang)

def _apply_rope(x, cos, sin):
    xf = x.astype(jnp.float32)
    x1, x2 = xf[..., 0::2], xf[..., 1::2]
    c, s = cos[None, :, None, :], sin[None, :, None, :]
    out = jnp.stack([x1 * c - x2 * s, x1 * s + x2 * c], axis=-1).reshape(x.shape)
    return out.astype(x.dtype)

def _block_attention(q, k, v):
    B, L, _, dh = q.shape
    nq = L // Q_BLOCK
    qb = q.reshape(B, nq, Q_BLOCK, ATT_KV_HEADS, ATT_GROUP, dh).transpose(1, 0, 3, 4, 2, 5)
    kt = k.transpose(0, 2, 1, 3)
    vt = v.transpose(0, 2, 1, 3)
    scale = dh ** -0.5

    def one_block(qblk):
        s = jnp.einsum('bhgqd,bhkd->bhgqk', qblk, kt).astype(jnp.float32) * scale
        p = jax.nn.softmax(s, axis=-1)
        return jnp.einsum('bhgqk,bhkd->bhgqd', p.astype(vt.dtype), vt)

    o = lax.map(one_block, qb)
    return o.transpose(1, 0, 4, 2, 3, 5).reshape(B, L, ATT_QW)

def _attention_group(u_q, u_k, u_v, q_norm_w, k_norm_w, out_norm_w):
    B, L, _ = u_q.shape
    q = _rmsnorm(u_q.reshape(B, L, ATT_HEADS, ATT_DH), q_norm_w)
    k = _rmsnorm(u_k.reshape(B, L, ATT_KV_HEADS, ATT_DH), k_norm_w)
    v = u_v.reshape(B, L, ATT_KV_HEADS, ATT_DH)
    cos, sin = _axial_rope_tables(L)
    q, k = _apply_rope(q, cos, sin), _apply_rope(k, cos, sin)
    o = _block_attention(q, k, v)
    return _rmsnorm(o, out_norm_w)

def setup_inputs(seed: int = 0) -> dict:
    key = jax.random.key(seed)
    ks = jax.random.split(key, 16)
    f32 = jnp.float32
    gain = lambda k, shape: 1.0 + 0.02 * jax.random.normal(k, shape, f32)
    return {
        "x": jax.random.normal(ks[0], (BATCH, SEQ, D_MODEL), f32),
        "norm1_w": gain(ks[1], (DEPTH, D_MODEL)),
        "w_in": jax.random.normal(ks[2], (DEPTH, D_MODEL, D_IN), f32) * D_MODEL ** -0.5,
        "lb_logits": 0.5 * jax.random.normal(ks[3], (2, DEPTH + 1, HG_KW), f32),
        "hg_norm_w": gain(ks[4], (DEPTH, HG_DV)),
        "q_norm_w": gain(ks[5], (DEPTH, ATT_DH)),
        "k_norm_w": gain(ks[6], (DEPTH, ATT_DH)),
        "att_norm_w": gain(ks[7], (DEPTH, ATT_QW)),
        "w_out": jax.random.normal(ks[8], (DEPTH, D_MIX, D_MODEL), f32) * D_MIX ** -0.5,
        "norm2_w": gain(ks[9], (DEPTH, D_MODEL)),
        "w_gate_up": jax.random.normal(ks[10], (DEPTH, D_MODEL, 2 * D_FF), f32) * D_MODEL ** -0.5,
        "w_down": jax.random.normal(ks[11], (DEPTH, D_FF, D_MODEL), f32) * D_FF ** -0.5,
        "final_norm_w": gain(ks[12], (D_MODEL,)),
    }

def reference(x, norm1_w, w_in, lb_logits, hg_norm_w, q_norm_w, k_norm_w, att_norm_w,
              w_out, norm2_w, w_gate_up, w_down, final_norm_w):
    lb_all = jnp.cumsum(jax.nn.softmax(lb_logits.astype(jnp.float32), axis=1), axis=1)
    splits = np.cumsum([HG_KW, HG_KW, HG_KW, HG_VW, HG_VW, ATT_QW, ATT_KVW]).tolist()
    for l in range(DEPTH):
        h = _rmsnorm(x, norm1_w[l])
        u = jnp.einsum('bld,de->ble', h, w_in[l])
        u_q, u_ff, u_fb, u_i, u_g, a_q, a_k, a_v = jnp.split(u, splits, axis=-1)
        o_hg = _hgrn2_group(u_q, u_ff, u_fb, u_i, u_g, lb_all[0, l], lb_all[1, l], hg_norm_w[l])
        o_att = _attention_group(a_q, a_k, a_v, q_norm_w[l], k_norm_w[l], att_norm_w[l])
        mix = jnp.concatenate([o_hg, o_att], axis=-1)
        x = x + jnp.einsum('ble,ed->bld', mix, w_out[l])
        h2 = _rmsnorm(x, norm2_w[l])
        gate, up = jnp.split(jnp.einsum('bld,df->blf', h2, w_gate_up[l]), 2, axis=-1)
        x = x + jnp.einsum('blf,fd->bld', jax.nn.silu(gate) * up, w_down[l])
    return _rmsnorm(x, final_norm_w)


_drawn_inputs = setup_inputs


def setup_inputs(seed=0):
    import zlib

    import numpy as np

    out = dict(_drawn_inputs(seed))
    spreads = {}
    factors = {'lb_logits': 3.491,
     'hg_norm_w': 7.853,
     'q_norm_w': 4.456,
     'k_norm_w': 4.398,
     'att_norm_w': 4.717,
     'norm2_w': 4.733,
     'final_norm_w': 2.893}
    for name, (base, spread) in spreads.items():
        noise = np.random.default_rng([zlib.crc32(name.encode()), seed]).standard_normal(out[name].shape)
        drawn = base * np.exp(spread * noise) if base else spread * noise
        out[name] = jnp.asarray(drawn.astype(out[name].dtype))
    for name, factor in factors.items():
        out[name] = (out[name] * factor).astype(out[name].dtype)
    return out
```

```python
import concourse.bass as bass
from concourse import mybir
from contextlib import ExitStack

FP32 = mybir.dt.float32
F32R = mybir.dt.float32r
ACT = mybir.ActivationFunctionType
ALU = mybir.AluOpType
AX = mybir.AxisListType

P = 128
L = 2048
D = 1024
KD = D // P
NT = L // P
BANK = 512
EPS = 1e-6

HG = 4
HGW = HG * P
CHUNK = 64
CPT = P // CHUNK
AH, KVH, DH = 8, 2, 64
GROUP = AH // KVH
AQW, AKW = AH * DH, KVH * DH
NS = AH + KVH

WB = 256
FEATURE_COLS = 3 * HGW
TOKEN_COLS = 2 * HGW + AQW + 2 * AKW
C_I, C_G, C_AQ, C_AK = 0, HGW, 2 * HGW, 2 * HGW + AQW

DFF = 2816
NF = DFF // P
HALF = L // 2
HT = HALF // P
SPLIT = 3


def f32(ap):
    return ap.bitcast(FP32)


def stage_semaphore(nc, sems, name):
    sems.append(nc.alloc_semaphore(name=name))
    return sems[-1]


def stage_block(nc, ctx, sems):
    def clear():
        nc.clear_and_free_semaphores(sems)
        nc.all_engine_barrier()

    ctx.callback(clear)
    return ctx.enter_context(nc.Block())


def split_products(nc, out, stationary, moving, steps):
    (s_hi, s_lo), (m_hi, m_lo) = stationary, moving
    for k in range(steps):
        nc.tensor.matmul(out, s_hi(k), m_hi(k), start=(k == 0), stop=False)
        nc.tensor.matmul(out, s_hi(k), m_lo(k), start=False, stop=False)
        last = nc.tensor.matmul(out, s_lo(k), m_hi(k), start=False, stop=(k == steps - 1))
    return last


def load_columns(rows):
    return rows.rearrange("(k p) n -> p k n", p=P)


def normalise_input(nc, const, hT_hi, hT_lo, x, norm1_w):
    ctx, sems = ExitStack(), []
    with ctx:
        def sb(name, shape, dt=FP32):
            return ctx.enter_context(nc.sbuf_tensor(name, shape, dt))

        def sem(name):
            return stage_semaphore(nc, sems, name)

        x_tile = [sb(f"x_tile{s}", [P, D]) for s in range(2)]
        h_tile = [sb(f"h_tile{s}", [P, D]) for s in range(2)]
        squares = sb("squares", [P, D])
        w_row = sb("norm1_row", [P, D])
        total = [sb(f"x_total{s}", [P, 1]) for s in range(2)]
        root = [sb(f"x_root{s}", [P, 1]) for s in range(2)]
        rstd = [sb(f"x_rstd{s}", [P, 1]) for s in range(2)]
        turned = [[ctx.enter_context(nc.psum_tensor(f"h_turned{s}{j}", [P, BANK], FP32)) for j in range(2)]
                  for s in range(2)]
        x_in = [sem(f"x_in{s}") for s in range(2)]
        w_in_s = sem("norm1_in")
        const_ready, zeroed = sem("const_ready"), sem("ident_zeroed")
        total_ready, root_ready, rstd_ready = sem("x_total_ready"), sem("x_root_ready"), sem("x_rstd_ready")
        h_ready, h_turned, hi_ready, lo_ready = sem("h_ready"), sem("h_turned"), sem("hT_hi_ready"), sem("hT_lo_ready")
        ident, eps = const["ident"], const["eps"]
        block = stage_block(nc, ctx, sems)

        @block.gpsimd
        def _(pool):
            nc.gpsimd.memset(ident[:, :], 0.0).then_inc(zeroed, 1)
            nc.gpsimd.memset(eps[:, :], EPS).then_inc(const_ready, 1)
            pool.wait_ge(zeroed, 1)
            nc.gpsimd.affine_select(out=ident[:, :], in_=ident[:, :], compare_op=ALU.not_equal, fill=1.0, base=0,
                                    pattern=[[-1, P]], channel_multiplier=1).then_inc(const_ready, 1)

        @block.sync
        def _(sp):
            sp.dma_start(w_row[:, :], norm1_w.partition_broadcast(P)).then_inc(w_in_s, 16)
            for s in range(2):
                sp.dma_start(x_tile[s][:, :], x[s * P:(s + 1) * P, :]).then_inc(x_in[s], 16)
            with sp.Fori(1, NT // 2) as i:
                for s in range(2):
                    sp.wait_ge(h_ready, 2 * i + s - 1)
                    sp.dma_start(x_tile[s][:, :], x[bass.ds(i * 2 * P + s * P, P), :]).then_inc(x_in[s], 16)

        @block.scalar
        def _(act):
            def statistics(i, s):
                act.wait_ge(x_in[s], 16 * i + 16)
                nc.scalar.activation(squares[:, :], x_tile[s][:, :], ACT.Square,
                                     accum_out=total[s][:, :]).then_inc(total_ready, 1)
                act.wait_ge(total_ready, 2 * i + s + 1)
                nc.scalar.activation(root[s][:, :], total[s][:, :], ACT.Sqrt, bias=eps[:, :],
                                     scale=1.0 / D).then_inc(root_ready, 1)

            def round_hi(n, s, t0):
                act.wait_ge(h_turned, n)
                for j in range(2):
                    nc.scalar.activation(hT_hi[:, 4 * j:4 * j + 4, bass.ds(t0, P)],
                                         turned[s][j][:, :].rearrange("p (k t) -> p k t", t=P),
                                         ACT.Copy).then_inc(hi_ready, 1)

            act.wait_ge(const_ready, 2)
            statistics(0, 0)
            statistics(0, 1)
            round_hi(1, 0, 0)
            with act.Fori(1, NT // 2) as i:
                statistics(i, 0)
                round_hi(2 * i, 1, i * 2 * P - P)
                statistics(i, 1)
                round_hi(2 * i + 1, 0, i * 2 * P)
            round_hi(NT, 1, L - P)

        @block.vector
        def _(dve):
            def scale(i, s, first):
                n = 2 * i + s + 1
                dve.wait_ge(root_ready, n)
                nc.vector.reciprocal(rstd[s][:, :], root[s][:, :]).then_inc(rstd_ready, 1)
                if not first:
                    dve.wait_ge(h_turned, 2 * i + s - 1)
                dve.wait_ge(rstd_ready, n)
                nc.vector.scalar_tensor_tensor(out=h_tile[s][:, :], in0=x_tile[s][:, :], scalar=rstd[s][:, :],
                                               in1=w_row[:, :], op0=ALU.mult, op1=ALU.mult).then_inc(h_ready, 1)

            def remainder(n, s, t0):
                for j in range(2):
                    dve.wait_ge(hi_ready, 2 * n - 1 + j)
                    nc.vector.tensor_sub(hT_lo[:, 4 * j:4 * j + 4, bass.ds(t0, P)],
                                         turned[s][j][:, :].rearrange("p (k t) -> p k t", t=P),
                                         f32(hT_hi[:, 4 * j:4 * j + 4, bass.ds(t0, P)])).then_inc(lo_ready, 1)

            dve.wait_ge(w_in_s, 16)
            scale(0, 0, True)
            scale(0, 1, True)
            remainder(1, 0, 0)
            with dve.Fori(1, NT // 2) as i:
                scale(i, 0, False)
                remainder(2 * i, 1, i * 2 * P - P)
                scale(i, 1, False)
                remainder(2 * i + 1, 0, i * 2 * P)
            remainder(NT, 1, L - P)

        @block.tensor
        def _(pe):
            def turn(i, s, first):
                pe.wait_ge(h_ready, 2 * i + s + 1)
                if not first:
                    pe.wait_ge(lo_ready, 4 * i + 2 * s - 2)
                for k in range(KD):
                    last = nc.tensor.transpose(turned[s][k // 4][:, (k % 4) * P:(k % 4 + 1) * P],
                                               h_tile[s][:, k * P:(k + 1) * P], ident[:, :])
                last.then_inc(h_turned, 1)

            pe.wait_ge(const_ready, 2)
            turn(0, 0, True)
            turn(0, 1, True)
            with pe.Fori(1, NT // 2) as i:
                turn(i, 0, False)
                turn(i, 1, False)


def project_input(nc, head_squares, hT_hi, hT_lo, w_in, lb_logits, q_scr, f_scr, k_scr, tok_scr):
    FB = FEATURE_COLS // WB
    NB = (FEATURE_COLS + TOKEN_COLS) // WB
    TB = L // BANK
    FU = 2 * TB
    ctx, sems = ExitStack(), []
    with ctx:
        def sb(name, shape, dt=FP32):
            return ctx.enter_context(nc.sbuf_tensor(name, shape, dt))

        def sem(name):
            return stage_semaphore(nc, sems, name)

        raw = [sb(f"w_raw{s}", [P, KD, WB]) for s in range(2)]
        w_hi = [sb(f"w_hi{s}", [P, KD, WB], F32R) for s in range(2)]
        w_lo = [sb(f"w_lo{s}", [P, KD, WB], F32R) for s in range(2)]
        sig = [[sb(f"sig{s}{j}", [P, BANK]) for j in range(2)] for s in range(2)]
        stage = [[sb(f"stage{s}{j}", [P, 2 * BANK]) for j in range(2)] for s in range(2)]
        logits, lb_exp = sb("lb_logits_sb", [P, 2, 2, HG]), sb("lb_exp", [P, 2, 2, HG])
        lb_work = sb("lb_work", [P, 3, 2, HG])
        lb, one_less = sb("lb", [P, 2 * HG]), sb("one_less_lb", [P, 2 * HG])
        ps = [ctx.enter_context(nc.psum_tensor(f"u_ps{b}", [P, BANK], FP32)) for b in range(8)]
        w_arrived = [sem(f"w_arrived{s}") for s in range(2)]
        w_hi_ready, w_split, w_slot_free = sem("w_hi_ready"), sem("w_split"), sem("w_slot_free")
        u_done, act_done, u_out = sem("u_done"), sem("u_act_done"), sem("u_out")
        stored = [sem(f"stored{s}") for s in range(2)]
        k_stored = [sem(f"k_stored{s}") for s in range(2)]
        lb_in, lb_step, lb_exped = sem("lb_in"), sem("lb_step"), sem("lb_exped")
        w_cols = load_columns(w_in)
        tok_rows = tok_scr.rearrange("(g t p) c -> g p t c", t=4, p=P)
        block = stage_block(nc, ctx, sems)

        def unit0(b):
            return b * FU if isinstance(b, int) and b < FB else FB * FU + (b - FB) * NT

        @block.sync
        def _(sp):
            def load(b, s):
                sp.dma_start(raw[s][:, :, :], w_cols[:, :, bass.ds(b * WB, WB)]).then_inc(w_arrived[s], 16)

            def load_after_split(b, s):
                sp.wait_ge(w_split, b - 1)
                load(b, s)

            def store_feature(b, with_k):
                for g in range(4):
                    f, half, s = g // 2, g % 2, g % 2
                    tile = 2 * b + f
                    cols = slice(half * 2 * BANK, (half + 1) * 2 * BANK)
                    sp.wait_ge(u_out, b * FU + 2 * g + 2)
                    if not with_k:
                        sp.dma_start(q_scr[tile, :, cols], stage[s][0][:, :]).then_inc(stored[s], 16)
                    else:
                        sp.dma_start(f_scr[bass.ds(tile - HG, 1), :, cols].rearrange("o p t -> (o p) t"),
                                     stage[s][0][:, :]).then_inc(stored[s], 16)
                        sp.dma_start(k_scr[bass.ds(tile - HG, 1), :, cols].rearrange("o p t -> (o p) t"),
                                     stage[s][1][:, :]).then_inc(k_stored[s], 16)

            def store_token(b):
                for g in range(4):
                    sp.wait_ge(u_out, unit0(b) + 4 * g + 4)
                    sp.dma_start(tok_rows[g, :, :, (b - FB) * WB:(b - FB + 1) * WB],
                                 stage[g % 2][0][:, :].rearrange("p (t c) -> p t c", t=4)).then_inc(stored[g % 2], 16)

            for j in range(2):
                for d in range(2):
                    sp.dma_start(logits[:, d, j, :], lb_logits[d, j, :].rearrange("(h p) -> p h", p=P),
                                 allow_slow_non_contiguous=True).then_inc(lb_in, 16)
            load(0, 0)
            load(1, 1)
            for b in range(2):
                load_after_split(b + 2, b)
                store_feature(b, False)
            with sp.Fori(1, FB // 2) as i:
                for s in range(2):
                    load_after_split(2 * i + s + 2, s)
                    store_feature(2 * i + s, True)
            for b in range(FB, NB):
                if b + 2 < NB:
                    load_after_split(b + 2, b % 2)
                store_token(b)
            for s in range(2):
                sp.wait_ge(stored[s], 16 * 2 * NB)
                sp.wait_ge(k_stored[s], 16 * 2 * (FB - 2))

        @block.gpsimd
        def _(pool):
            def split(b, s, used):
                pool.wait_ge(w_arrived[s], 16 + 8 * (b - s))
                if used is not None:
                    pool.wait_ge(u_done, used)
                pool.sem_inc(w_slot_free, 1)
                nc.gpsimd.tensor_copy(w_hi[s][:, :, :], raw[s][:, :, :]).then_inc(w_hi_ready, 1)
                pool.wait_ge(w_hi_ready, b + 1)
                nc.gpsimd.tensor_sub(w_lo[s][:, :, :], raw[s][:, :, :], f32(w_hi[s][:, :, :])).then_inc(w_split, 1)

            split(0, 0, None)
            split(1, 1, None)
            with pool.Fori(1, FB // 2 + 1) as i:
                split(2 * i, 0, (2 * i - 1) * FU)
                split(2 * i + 1, 1, 2 * i * FU)
            for b in range(FB + 2, NB):
                split(b, b % 2, unit0(b - 1))

        @block.tensor
        def _(pe):
            def feature_block(b, s, first):
                pe.wait_ge(w_split, b + 1)
                for f in range(2):
                    for tb in range(TB):
                        if not first:
                            pe.wait_ge(u_out, b * FU + TB * f + tb - 7)
                        cols = slice(tb * BANK, (tb + 1) * BANK)
                        split_products(
                            nc, ps[TB * f + tb][:, :],
                            (lambda k: w_hi[s][:, k, f * P:(f + 1) * P], lambda k: w_lo[s][:, k, f * P:(f + 1) * P]),
                            (lambda k: hT_hi[:, k, cols], lambda k: hT_lo[:, k, cols]), KD).then_inc(u_done, 1)

            def token_block(b, s):
                pe.wait_ge(w_split, b + 1)
                for t in range(NT):
                    pe.wait_ge(u_out, b * NT - FB * (NT - FU) + t - 7)
                    toks = slice(t * P, (t + 1) * P)
                    split_products(
                        nc, ps[t % 8][:, 0:WB],
                        (lambda k: hT_hi[:, k, toks], lambda k: hT_lo[:, k, toks]),
                        (lambda k: w_hi[s][:, k, :], lambda k: w_lo[s][:, k, :]), KD).then_inc(u_done, 1)

            feature_block(0, 0, True)
            feature_block(1, 1, False)
            with pe.Fori(1, FB // 2) as i:
                feature_block(2 * i, 0, False)
                feature_block(2 * i + 1, 1, False)
            with pe.Fori(FB // 2, NB // 2) as i:
                token_block(2 * i, 0)
                token_block(2 * i + 1, 1)
            token_block(NB - 1, (NB - 1) % 2)

        @block.scalar
        def _(act):
            def feature_units(b, both, first):
                for n in range(FU):
                    act.wait_ge(u_done, b * FU + n + 1)
                    if not first or n >= 2:
                        act.wait_ge(u_out, b * FU + n - 1)
                    ins = nc.scalar.activation(sig[n % 2][0][:, :], ps[n][:, :], ACT.Sigmoid)
                    if both:
                        ins = nc.scalar.activation(sig[n % 2][1][:, :], ps[n][:, :], ACT.Sigmoid, scale=-1.0)
                    ins.then_inc(act_done, 1)

            def token_units(b, func):
                for t in range(NT):
                    n = unit0(b) + t
                    act.wait_ge(u_done, n + 1)
                    act.wait_ge(u_out, n - 1)
                    nc.scalar.activation(sig[t % 2][0][:, 0:WB], ps[t % 8][:, 0:WB], func).then_inc(act_done, 1)

            act.wait_ge(lb_step, 2)
            nc.scalar.activation(lb_exp[:, :, :, :], logits[:, :, :, :], ACT.Exp).then_inc(lb_exped, 1)
            feature_units(0, False, True)
            feature_units(1, False, False)
            with act.Fori(1, FB // 2) as i:
                feature_units(2 * i, True, False)
                feature_units(2 * i + 1, True, False)
            for b in range(FB + 2, FB + 4):
                token_units(b, ACT.Sigmoid)
            for b in range(FB + 4, NB):
                token_units(b, ACT.Square)

        @block.vector
        def _(dve):
            l0, l1 = logits[:, :, 0, :], logits[:, :, 1, :]
            top, total, inverse = (lb_work[:, j, :, :] for j in range(3))
            dve.wait_ge(lb_in, 64)
            nc.vector.tensor_max(top, l0, l1).then_inc(lb_step, 1)
            dve.wait_ge(lb_step, 1)
            nc.vector.tensor_sub(l0, l0, top)
            nc.vector.tensor_sub(l1, l1, top).then_inc(lb_step, 1)
            dve.wait_ge(lb_exped, 1)
            nc.vector.tensor_add(total, lb_exp[:, :, 0, :], lb_exp[:, :, 1, :]).then_inc(lb_step, 1)
            dve.wait_ge(lb_step, 3)
            nc.vector.reciprocal(inverse, total).then_inc(lb_step, 1)
            dve.wait_ge(lb_step, 4)
            nc.vector.tensor_mul(lb[:, :].rearrange("p (d h) -> p d h", h=HG), lb_exp[:, :, 0, :],
                                 inverse).then_inc(lb_step, 1)
            dve.wait_ge(lb_step, 5)
            nc.vector.tensor_scalar(one_less[:, :], lb[:, :], -1.0, 1.0, ALU.mult, ALU.add).then_inc(lb_step, 1)
            dve.wait_ge(lb_step, 6)

            def feature_units(b, gates, first):
                for n in range(FU):
                    g, tile = n // 2, 2 * b + n // TB
                    s, cols = g % 2, slice((n % 2) * BANK, (n % 2 + 1) * BANK)
                    dve.wait_ge(act_done, b * FU + n + 1)
                    if n % 2 == 0 and (not first or g >= 2):
                        dve.wait_ge(stored[s], 32 * b + 16 * (g // 2))
                    if not gates:
                        nc.vector.tensor_mul(stage[s][0][:, cols], ps[n][:, :], sig[n % 2][0][:, :]).then_inc(u_out, 1)
                    else:
                        col = bass.ds(tile - HG, 1)
                        nc.vector.tensor_scalar(stage[s][0][:, cols], sig[n % 2][0][:, :], one_less[:, col], lb[:, col],
                                                ALU.mult, ALU.add)
                        if n % 2 == 0:
                            dve.wait_ge(k_stored[s], 32 * (b - 2) + 16 * (g // 2) + 16)
                        nc.vector.tensor_scalar(stage[s][1][:, cols], sig[n % 2][1][:, :], one_less[:, col], None,
                                                ALU.mult).then_inc(u_out, 1)

            def token_units(b, kind, heads):
                for t in range(NT):
                    g = t // 4
                    s, cols = g % 2, slice((t % 4) * WB, (t % 4 + 1) * WB)
                    if kind == "copy":
                        dve.wait_ge(u_done, unit0(b) + t + 1)
                    else:
                        dve.wait_ge(act_done, unit0(b) + t + 1 - 2 * NT)
                    if t % 4 == 0:
                        dve.wait_ge(stored[s], 32 * b + 16 * (g // 2))
                    out = stage[s][0][:, cols]
                    if kind == "copy":
                        nc.vector.tensor_copy(out, ps[t % 8][:, 0:WB]).then_inc(u_out, 1)
                    elif kind == "silu":
                        nc.vector.tensor_mul(out, ps[t % 8][:, 0:WB], sig[t % 2][0][:, 0:WB]).then_inc(u_out, 1)
                    else:
                        n = (heads.stop - heads.start)
                        nc.vector.tensor_copy(out, ps[t % 8][:, 0:WB])
                        nc.vector.tensor_reduce(head_squares[:, t, heads],
                                                sig[t % 2][0][:, 0:n * DH].rearrange("p (h c) -> p h c", c=DH),
                                                AX.X, ALU.add).then_inc(u_out, 1)

            for s in range(2):
                dve.sem_inc(k_stored[s], 16)
            feature_units(0, False, True)
            feature_units(1, False, False)
            with dve.Fori(1, FB // 2) as i:
                feature_units(2 * i, True, False)
                feature_units(2 * i + 1, True, False)
            for b, kind, heads in [(0, "copy", None), (1, "copy", None), (2, "silu", None), (3, "silu", None),
                                   (4, "squares", slice(0, 4)), (5, "squares", slice(4, 8)),
                                   (6, "squares", slice(8, 10))]:
                token_units(FB + b, kind, heads)


def wait_for(eng, sem, value):
    if not isinstance(value, int) or value > 0:
        eng.wait_ge(sem, value)


def pass_waits(eng, steps):
    eng.sem_inc(steps, 1)


def flat(t):
    return t[:, :, :].rearrange("p h t -> p (h t)")


def recurrence(nc, const, forward, o_back, o_squares, q_scr, f_scr, k_scr, tok_scr, mix_scr):
    way = "forward" if forward else "back"
    ctx, sems = ExitStack(), []
    with ctx:
        def sb(name, shape, dt=FP32):
            return [ctx.enter_context(nc.sbuf_tensor(f"{way}_{name}{s}", shape, dt)) for s in range(2)]

        def pb(name, n):
            return [ctx.enter_context(nc.psum_tensor(f"{way}_{name}{s}", [P, BANK], FP32)) for s in range(n)]

        def sem(name):
            return stage_semaphore(nc, sems, f"{way}_{name}")

        q, f, k = sb("r_q", [P, HG, P]), sb("r_f", [P, HG, P]), sb("r_k", [P, HG, P])
        v = sb("r_v", [P, HGW])
        log_f, b, b_mid, b_end = (sb(x, [P, HG * P]) for x in ("log_f", "b", "b_mid", "b_end"))
        e_in, e_key, e_out, e_b = (sb(x, [P, HG * P]) for x in ("e_in", "e_key", "e_out", "e_b"))
        q_in, k_in, k_out, q_out = (sb(x, [P, HG, P]) for x in ("q_inner", "k_inner", "k_outer", "q_outer"))
        k_turned = sb("k_turned", [P, HG, P])
        scores = sb("scores", [P, HG, CHUNK])
        o_tile, squares = sb("o_tile", [P, HGW]), sb("o_sq", [P, HGW])
        state = [ctx.enter_context(nc.sbuf_tensor(f"{way}_state{m}", [P, HG, P], FP32)) for m in range(2 * CPT)]
        keep = ctx.enter_context(nc.sbuf_tensor(f"{way}_keep", [P, HG, CHUNK], mybir.dt.int32))
        restart = ctx.enter_context(nc.sbuf_tensor(f"{way}_restart", [P, HG * P], FP32))
        ps_turn, ps_scores, ps_add, ps_o = pb("ps_turn", 1), pb("ps_scores", 1), pb("ps_add", 2), pb("ps_o", 2)
        q_here, f_here, k_here, v_here = ([sem(f"{x}_here{s}") for s in range(2)] for x in "qfkv")
        logs, cums, exps = sem("log_f_ready"), sem("cumulative_ready"), sem("exponentials_ready")
        q_in_ready, q_out_ready, k_ready = sem("q_in_ready"), sem("q_out_ready"), sem("k_in_out_ready")
        turned, turned_copied = sem("k_turned_psum"), sem("k_turned_ready")
        scored, masked = sem("scores_done"), sem("scores_masked")
        added, state_ready = sem("state_addend_done"), sem("state_ready")
        o_done, o_out = sem("o_done"), sem("o_out")
        o_stored = [sem(f"o_stored{s}") for s in range(2)]
        squared, prepared, zeroed = sem("o_squared"), sem("constants_ready"), sem("constants_zeroed")
        sp_steps, dve_steps = sem("sp_steps"), sem("dve_steps")
        order = (0, 1) if forward else (1, 0)
        mid, end = (CHUNK // 2 - 1, CHUNK - 1) if forward else (CHUNK // 2, 0)
        d = 0 if forward else 1
        block = stage_block(nc, ctx, sems)

        def first_token(n):
            return n * P if forward else L - P - n * P

        def in_order(ap):
            return ap if forward else ap[:, ::-1]

        def chunks(ap):
            return ap.rearrange("p (c t) -> p c t", t=CHUNK)

        def at_chunk(ap, t):
            return chunks(ap)[:, :, t:t + 1].to_broadcast([P, HG * CPT, CHUNK])

        def iterations(eng, core, scoring, gates, squares_of=lambda n, s: None):
            def iteration(n, s):
                if not isinstance(n, int) or 1 <= n:
                    core(n - 1, 1 - s)
                if not isinstance(n, int) or n < NT:
                    scoring(n, s)
                if not isinstance(n, int) or n + 1 < NT:
                    gates(n + 1, 1 - s)
                if not isinstance(n, int) or 1 <= n:
                    squares_of(n - 1, 1 - s)

            gates(0, 0)
            for n in range(3):
                iteration(n, n % 2)
            with eng.Fori(0, (NT - 4) // 2) as i:
                iteration(2 * i + 3, 1)
                iteration(2 * i + 4, 0)
            iteration(NT - 1, 1)
            iteration(NT, 0)

        @block.sync
        def _(sp):
            def load(n, s):
                cols = bass.ds(first_token(n), P)
                for scr, tile, here, used, value in (
                        (f_scr[d * HG:(d + 1) * HG], f[s], f_here[s], logs, n - 1),
                        (q_scr, q[s], q_here[s], q_out_ready, n - 1),
                        (k_scr[d * HG:(d + 1) * HG], k[s], k_here[s], k_ready, 2 * n - 2)):
                    wait_for(sp, used, value)
                    pass_waits(sp, sp_steps)
                    sp.dma_start(tile[:, :, :], scr.rearrange("h p t -> p h t")[:, :, cols]).then_inc(here, 16)
                wait_for(sp, o_done, n - 1)
                pass_waits(sp, sp_steps)
                sp.dma_start(v[s][:, :], tok_scr[cols, C_I:C_I + HGW]).then_inc(v_here[s], 16)

            def store(n, s):
                rows = bass.ds(first_token(n), P)
                sp.wait_ge(o_out, n + 1)
                sp.dma_start(mix_scr[rows, 0:HGW], o_tile[s][:, :]).then_inc(o_stored[s], 16)

            load(0, 0)
            load(1, 1)
            with sp.Fori(1, NT // 2) as i:
                for s in range(2):
                    load(2 * i + s, s)
                    if forward:
                        store(2 * i + s - 2, s)
            if forward:
                for n in range(NT - 2, NT):
                    store(n, n % 2)
                for s in range(2):
                    sp.wait_ge(o_stored[s], 8 * NT)

        @block.gpsimd
        def _(pool):
            nc.gpsimd.memset(keep[:, :, :], 1).then_inc(zeroed, 1)
            nc.gpsimd.memset(restart[:, :], 1.0).then_inc(zeroed, 1)
            for s in range(2):
                nc.gpsimd.memset(scores[s][:, :, :], 0.0).then_inc(zeroed, 1)
            nc.gpsimd.memset(state[0][:, :, :], 0.0).then_inc(zeroed, 1)
            pool.wait_ge(zeroed, 5)
            nc.gpsimd.memset(chunks(restart[:, :])[:, :, 0:1], 0.0).then_inc(prepared, 1)
            for c in range(CPT):
                pool.wait_ge(prepared, 1 + c)
                half, sign = keep[c * CHUNK:(c + 1) * CHUNK, :, :], 1 if forward else -1
                nc.gpsimd.affine_select(out=half, in_=half, compare_op=ALU.is_ge, fill=0, base=0,
                                        pattern=[[0, HG], [sign, CHUNK]], channel_multiplier=-sign).then_inc(prepared, 1)

            def gates(n, s):
                pool.wait_ge(k_here[s], 8 * (n - s) + 16)
                pool.wait_ge(exps, 4 * n + 2)
                wait_for(pool, scored, n - 1)
                nc.gpsimd.tensor_mul(flat(k_in[s]), flat(k[s]), e_key[s][:, :]).then_inc(k_ready, 1)
                pool.wait_ge(exps, 4 * n + 3)
                wait_for(pool, turned, n - 1)
                nc.gpsimd.tensor_mul(flat(k_out[s]), flat(k[s]), e_out[s][:, :]).then_inc(k_ready, 1)

            iterations(pool, lambda n, s: None, lambda n, s: None, gates)

        @block.scalar
        def _(act):
            def square(n, s):
                if forward:
                    act.wait_ge(o_out, n + 1)
                    for h in range(HG):
                        ins = nc.scalar.activation(squares[s][:, h * P:(h + 1) * P], o_tile[s][:, h * P:(h + 1) * P],
                                                   ACT.Square, accum_out=o_squares[:, bass.ds(n, 1), h:h + 1])
                    ins.then_inc(squared, 1)

            def scoring(n, s):
                act.wait_ge(turned, n + 1)
                wait_for(act, added, 2 * n - 2)
                nc.scalar.activation(flat(k_turned[s]), ps_turn[0][:, :], ACT.Copy).then_inc(turned_copied, 1)

            def gates(n, s):
                act.wait_ge(f_here[s], 8 * (n - s) + 16)
                wait_for(act, cums, 3 * n - 5)
                nc.scalar.activation(log_f[s][:, :], flat(f[s]), ACT.Ln).then_inc(logs, 1)
                act.wait_ge(cums, 3 * n + 2)
                wait_for(act, q_in_ready, n - 1)
                wait_for(act, k_ready, 2 * n - 2)
                nc.scalar.activation(e_in[s][:, :], b_mid[s][:, :], ACT.Exp).then_inc(exps, 1)
                nc.scalar.activation(e_key[s][:, :], b_mid[s][:, :], ACT.Exp, scale=-1.0).then_inc(exps, 1)
                act.wait_ge(cums, 3 * n + 3)
                nc.scalar.activation(e_out[s][:, :], b_end[s][:, :], ACT.Exp).then_inc(exps, 1)
                wait_for(act, q_out_ready, n - 1)
                wait_for(act, state_ready, 2 * n - 2)
                nc.scalar.activation(e_b[s][:, :], b[s][:, :], ACT.Exp).then_inc(exps, 1)

            iterations(act, lambda n, s: None, scoring, gates, square)

        @block.vector
        def _(dve):
            def update_states(n, s):
                for c in range(CPT):
                    m, lo = 2 * s + c, order[c] * CHUNK
                    dve.wait_ge(added, 2 * n + c + 1)
                    wait_for(dve, state_ready, 2 * n + c)
                    wait_for(dve, o_done, n - 1 + c)
                    for h in range(HG):
                        col = h * P + lo + end
                        last = nc.vector.scalar_tensor_tensor(
                            out=state[(m + 1) % 4][:, h, :], in0=state[m][:, h, :], scalar=e_b[s][:, col:col + 1],
                            in1=ps_add[c][:, h * P:(h + 1) * P], op0=ALU.mult, op1=ALU.add)
                    last.then_inc(state_ready, 1)

            def take_output(n, s):
                dve.wait_ge(o_done, n + 1)
                pass_waits(dve, dve_steps)
                t = n if forward else NT - 1 - n
                back = o_back[:, bass.ds(t, 1), :].rearrange("p o c -> p (o c)")
                if forward:
                    wait_for(dve, o_stored[s], 8 * (n - s))
                    wait_for(dve, squared, n - 1)
                    nc.vector.tensor_add(o_tile[s][:, :], ps_o[s][:, :], back).then_inc(o_out, 1)
                else:
                    nc.vector.tensor_copy(back, ps_o[s][:, :]).then_inc(o_out, 1)

            def cumulate(n, s):
                dve.wait_ge(logs, n + 1)
                wait_for(dve, exps, 4 * n - 4)
                nc.vector.tensor_tensor_scan(in_order(b[s][:, :]), restart[:, :], in_order(log_f[s][:, :]), 0.0,
                                             ALU.mult, ALU.add).then_inc(cums, 1)
                dve.wait_ge(cums, 3 * n + 1)
                nc.vector.tensor_sub(chunks(b_mid[s][:, :]), chunks(b[s][:, :]), at_chunk(b[s][:, :], mid)).then_inc(cums, 1)
                nc.vector.tensor_sub(chunks(b_end[s][:, :]), at_chunk(b[s][:, :], end), chunks(b[s][:, :])).then_inc(cums, 1)

            def query_in(n, s):
                dve.wait_ge(q_here[s], 8 * (n - s) + 16)
                dve.wait_ge(exps, 4 * n + 1)
                wait_for(dve, scored, n - 1)
                nc.vector.tensor_mul(flat(q_in[s]), flat(q[s]), e_in[s][:, :]).then_inc(q_in_ready, 1)

            def query_out(n, s):
                dve.wait_ge(exps, 4 * n + 4)
                wait_for(dve, o_done, n - 1)
                nc.vector.tensor_mul(flat(q_out[s]), flat(q[s]), e_b[s][:, :]).then_inc(q_out_ready, 1)

            def mask(n, s):
                nc.vector.copy_predicated(scores[s][:, :, :], keep[:, :, :],
                                          ps_scores[0][:, 0:HG * CHUNK].rearrange("p (h t) -> p h t", t=CHUNK)).then_inc(masked, 1)

            def iteration(n, s):
                every = not isinstance(n, int)
                if every or n >= 1:
                    update_states(n - 1, 1 - s)
                if every or n + 1 < NT:
                    cumulate(n + 1, 1 - s)
                if every or n >= 1:
                    take_output(n - 1, 1 - s)
                if every or n + 1 < NT:
                    query_in(n + 1, 1 - s)
                if every or n < NT:
                    dve.wait_ge(scored, n + 1)
                    wait_for(dve, o_done, n - 1)
                if every or n + 1 < NT:
                    query_out(n + 1, 1 - s)
                if every or n < NT:
                    mask(n, s)

            dve.wait_ge(prepared, 1 + CPT)
            cumulate(0, 0)
            query_in(0, 0)
            query_out(0, 0)
            for n in range(3):
                iteration(n, n % 2)
            with dve.Fori(0, (NT - 4) // 2) as i:
                iteration(2 * i + 3, 1)
                iteration(2 * i + 4, 0)
            iteration(NT - 1, 1)
            iteration(NT, 0)

        @block.tensor
        def _(pe):
            def core(n, s):
                pe.wait_ge(v_here[s], 8 * (n - s) + 16)
                pe.wait_ge(turned_copied, n + 1)
                for c in range(CPT):
                    half = slice(order[c] * CHUNK, (order[c] + 1) * CHUNK)
                    wait_for(pe, state_ready, 2 * n - 1 + c)
                    for h in range(HG):
                        last = nc.tensor.matmul(ps_add[c][:, h * P:(h + 1) * P], k_turned[s][half, h, :],
                                                v[s][half, h * P:(h + 1) * P], start=True, stop=True)
                    last.then_inc(added, 1)
                pe.wait_ge(masked, n + 1)
                pe.wait_ge(q_out_ready, n + 1)
                wait_for(pe, o_out, n - 1)
                for c in range(CPT):
                    half = slice(order[c] * CHUNK, (order[c] + 1) * CHUNK)
                    wait_for(pe, state_ready, 2 * n + c)
                    for h in range(HG):
                        cols = slice(h * P, (h + 1) * P)
                        nc.tensor.matmul(ps_o[s][half, cols], q_out[s][:, h, half], state[2 * s + c][:, h, :],
                                         start=True, stop=False)
                        last = nc.tensor.matmul(ps_o[s][half, cols], scores[s][half, h, :], v[s][half, cols],
                                                start=False, stop=True)
                last.then_inc(o_done, 1)

            def scoring(n, s):
                pe.wait_ge(k_ready, 2 * n + 2)
                wait_for(pe, turned_copied, n)
                for h in range(HG):
                    last = nc.tensor.transpose(ps_turn[0][:, h * P:(h + 1) * P], k_out[s][:, h, :], const["ident"][:, :])
                last.then_inc(turned, 1)
                pe.wait_ge(q_in_ready, n + 1)
                wait_for(pe, masked, n)
                for c in range(CPT):
                    half = slice(c * CHUNK, (c + 1) * CHUNK)
                    for h in range(HG):
                        last = nc.tensor.matmul(ps_scores[0][half, h * CHUNK:(h + 1) * CHUNK], k_in[s][:, h, half],
                                                q_in[s][:, h, half], start=True, stop=True)
                last.then_inc(scored, 1)

            pe.wait_ge(prepared, 1 + CPT)
            iterations(pe, core, scoring, lambda n, s: None)


def rotate(eng, nc, out, src, cos, sin, work, steps, at, shape):
    even, odd = src[..., 0::2], src[..., 1::2]
    cos, sin = cos.to_broadcast(shape), sin.to_broadcast(shape)
    for w, a, b in ((0, even, cos), (1, odd, sin), (2, even, sin), (3, odd, cos)):
        eng.tensor_mul(work[w], a, b).then_inc(steps, 1)
    eng.wait_ge(steps, at + 2)
    eng.tensor_sub(out[..., 0::2], work[0], work[1]).then_inc(steps, 1)
    eng.wait_ge(steps, at + 4)
    eng.tensor_add(out[..., 1::2], work[2], work[3]).then_inc(steps, 1)
    return at + 6


def prepare_keys(nc, const, head_squares, head_rstd, rope_sb, k_turned, v_split, k_norm_w, rope, tok_scr):
    ctx, sems = ExitStack(), []
    with ctx:
        def sb(name, shape, dt=FP32):
            return ctx.enter_context(nc.sbuf_tensor(name, shape, dt))

        def sem(name):
            return stage_semaphore(nc, sems, name)

        HALVES = 2
        keys, values = sb("keys", [P, NT, KVH, DH]), sb("values", [P, NT, KVH, DH])
        scaled, rotated = sb("k_scaled", [P, NT, KVH, DH]), sb("k_rotated", [P, NT, KVH, DH])
        work = [sb(f"k_work{w}", [P, NT, KVH, DH // 2]) for w in range(4)]
        k_split = sb("k_split", [P, NT, KVH, 2, DH])
        w_row, root = sb("k_norm_row", [P, DH]), sb("head_root", [P, NT, NS])
        ps = [ctx.enter_context(nc.psum_tensor(f"k_ps{b}", [P, BANK], FP32)) for b in range(8)]
        loaded, v_in, rooted, steps = sem("k_loaded"), sem("v_in"), sem("head_root_ready"), sem("k_steps")
        v_hi_ready, turned, copied = sem("v_hi_ready"), sem("k_turned_done"), sem("k_copied")
        block = stage_block(nc, ctx, sems)
        rows = tok_scr.rearrange("(t p) c -> p t c", p=P)

        @block.sync
        def _(sp):
            sp.dma_start(w_row[:, :], k_norm_w.partition_broadcast(P)).then_inc(loaded, 16)
            for j in range(2):
                sp.dma_start(rope_sb[:, j, :, :], rope[j].rearrange("(t p) c -> p t c", p=P)).then_inc(loaded, 16)
            sp.dma_start(keys[:, :, :, :].rearrange("p t h c -> p t (h c)"), rows[:, :, C_AK:C_AK + AKW]).then_inc(loaded, 16)
            sp.dma_start(values[:, :, :, :].rearrange("p t h c -> p t (h c)"),
                         rows[:, :, C_AK + AKW:TOKEN_COLS]).then_inc(v_in, 16)

        @block.scalar
        def _(act):
            nc.scalar.activation(root[:, :, :], head_squares[:, :, :], ACT.Sqrt, bias=const["eps"][:, :],
                                 scale=1.0 / DH).then_inc(rooted, 1)
            for b in range(8):
                act.wait_ge(turned, b + 1)
                t0 = 4 * (b % 4)
                nc.scalar.activation(k_turned[:, b // 4, t0 * P:(t0 + 4) * P], ps[b][:, :], ACT.Copy).then_inc(copied, 1)

        @block.gpsimd
        def _(pool):
            pool.wait_ge(v_in, 16)
            nc.gpsimd.tensor_copy(v_split[:, :, :, 0:DH], values[:, :, :, :]).then_inc(v_hi_ready, 1)
            pool.wait_ge(v_hi_ready, 1)
            nc.gpsimd.tensor_sub(v_split[:, :, :, DH:2 * DH], values[:, :, :, :], f32(v_split[:, :, :, 0:DH]))

        @block.vector
        def _(dve):
            dve.wait_ge(rooted, 1)
            nc.vector.reciprocal(head_rstd[:, :, :], root[:, :, :]).then_inc(steps, 1)
            dve.wait_ge(loaded, 64)
            dve.wait_ge(steps, 1)
            nc.vector.tensor_mul(scaled[:, :, :, :], keys[:, :, :, :],
                                 head_rstd[:, :, AH:NS].unsqueeze(3).to_broadcast([P, NT, KVH, DH])).then_inc(steps, 1)
            dve.wait_ge(steps, 2)
            flat_heads = scaled[:, :, :, :].rearrange("p t h c -> p (t h) c")
            nc.vector.tensor_mul(flat_heads, flat_heads,
                                 w_row[:, :].unsqueeze(1).to_broadcast([P, NT * KVH, DH])).then_inc(steps, 1)
            dve.wait_ge(steps, 3)
            at = rotate(dve, nc, rotated[:, :, :, :], scaled[:, :, :, :], rope_sb[:, 0, :, :].unsqueeze(2),
                        rope_sb[:, 1, :, :].unsqueeze(2), [w[:, :, :, :] for w in work], steps, 3,
                        [P, NT, KVH, DH // 2])
            dve.wait_ge(steps, at)
            nc.vector.tensor_copy(k_split[:, :, :, 0, :].bitcast(F32R), rotated[:, :, :, :]).then_inc(steps, 1)
            dve.wait_ge(steps, at + 1)
            nc.vector.tensor_sub(k_split[:, :, :, 1, :].bitcast(F32R), rotated[:, :, :, :],
                                 k_split[:, :, :, 0, :]).then_inc(steps, 1)

        @block.tensor
        def _(pe):
            pe.wait_ge(steps, 11)
            for b in range(8):
                for t in range(4):
                    last = nc.tensor.transpose(ps[b][:, t * P:(t + 1) * P],
                                               k_split[:, 4 * (b % 4) + t, b // 4, :, :].rearrange("p a c -> p (a c)"),
                                               const["ident"][:, :])
                last.then_inc(turned, 1)


def attention(nc, const, head_rstd, rope_sb, k_turned, v_split, att_squares, q_norm_w, tok_scr, mix_scr):
    ctx, sems = ExitStack(), []
    with ctx:
        def sb(name, shape, dt=FP32):
            return ctx.enter_context(nc.sbuf_tensor(name, shape, dt))

        def pb(name, banks=1):
            return ctx.enter_context(nc.psum_tensor(name, [P, banks * BANK], FP32))

        def sem(name):
            return stage_semaphore(nc, sems, name)

        NG = AH // GROUP
        SCALE = float(DH) ** -0.5
        w_row = sb("q_norm_row", [P, DH])
        q_raw, q_scaled = sb("q_raw", [P, AH, DH]), sb("q_scaled", [P, AH, DH])
        q_rotated = sb("q_rotated", [P, AH, DH])
        q_work = [sb(f"q_work{w}", [P, AH, DH // 2]) for w in range(4)]
        q_twice = [sb(f"q_twice_{x}", [P, AH, 2, DH]) for x in ("hi", "lo")]
        q_turned = [sb(f"q_turned_{x}", [P, AH, P], F32R) for x in ("hi", "lo")]
        probs = [sb(f"probs{s}", [P, L]) for s in range(2)]
        probs_hi, probs_lo = (sb(f"probs_{x}", [P, NT, GROUP, P], F32R) for x in ("hi", "lo"))
        half_max = [sb(f"half_max{s}", [P, 2]) for s in range(2)]
        less_max = [sb(f"less_max{s}", [P, 1]) for s in range(2)]
        half_sums = [sb(f"half_sums{g}", [P, GROUP, 2]) for g in range(NG)]
        sums, inverse = [sb(f"sums{g}", [P, GROUP]) for g in range(NG)], [sb(f"inverse{g}", [P, GROUP]) for g in range(NG)]
        o_turned = sb("att_o_turned", [P, GROUP * P])
        o_parts = [sb(f"o_parts{g}", [P, GROUP, 2 * DH]) for g in range(NG)]
        o_sum, o_att, squares = sb("o_sum", [P, GROUP, DH]), sb("o_att", [P, AQW]), sb("att_sq", [P, AQW])
        ps_s = [pb(f"ps_s{h}", 2) for h in range(2)]
        ps_t, ps_o, ps_x = [pb(f"ps_t{b}") for b in range(2)], pb("ps_pv"), pb("ps_x")
        w_here, q_here, q_used, pool_steps, pool_marks = (sem(x) for x in (
            "q_norm_here", "q_here", "q_used", "q_steps", "pool_marks"))
        scored, halved, max_ready, exp_done = (sem(x) for x in ("att_scored", "half_max_done", "less_max_ready", "exp_done"))
        turned, hi_ready, lo_ready = sem("probs_turned"), sem("probs_hi_ready"), sem("probs_lo_ready")
        multiplied, o_copied = sem("pv_done"), sem("o_copied")
        x_filled, x_copied = sem("x_filled"), sem("x_copied")
        summed, inverted = sem("sums_ready"), sem("inverse_ready")
        o_steps, o_ready, squared, stored = sem("o_sum_ready"), sem("o_att_ready"), sem("att_squared"), sem("att_stored")
        block = stage_block(nc, ctx, sems)

        def fill(t, j):
            return 6 * t + 1 + j

        def tiles(eng, body):
            body(0, True, False)
            with eng.Fori(1, NT - 1) as t:
                body(t, False, False)
            body(NT - 1, False, True)

        @block.sync
        def _(sp):
            sp.dma_start(w_row[:, :], q_norm_w.partition_broadcast(P)).then_inc(w_here, 16)
            sp.dma_start(flat(q_raw), tok_scr[0:P, C_AQ:C_AQ + AQW]).then_inc(q_here, 16)

            def body(t, first, last):
                if not last:
                    sp.wait_ge(q_used, t + 1)
                    sp.dma_start(flat(q_raw), tok_scr[bass.ds(t * P + P, P), C_AQ:C_AQ + AQW]).then_inc(q_here, 16)
                if not first:
                    sp.wait_ge(o_ready, 2 * t)
                    sp.dma_start(mix_scr[bass.ds(t * P - P, P), HGW:D], o_att[:, :]).then_inc(stored, 16)

            tiles(sp, body)
            sp.wait_ge(o_ready, 2 * NT)
            sp.dma_start(mix_scr[L - P:L, HGW:D], o_att[:, :]).then_inc(stored, 16)
            sp.wait_ge(stored, 16 * NT)

        @block.gpsimd
        def _(pool):
            STEPS = 10

            def prepare(t):
                at = t * STEPS
                rstd = head_rstd[:, bass.ds(t, 1), 0:AH].rearrange("p o h -> p (o h)")
                cos, sin = (rope_sb[:, j, bass.ds(t, 1), :] for j in range(2))
                pool.wait_ge(q_here, 16 * t + 16)
                nc.gpsimd.tensor_mul(q_scaled[:, :, :], q_raw[:, :, :],
                                     rstd.unsqueeze(2).to_broadcast([P, AH, DH])).then_inc(q_used, 1)
                pool.wait_ge(q_used, t + 1)
                nc.gpsimd.tensor_mul(q_scaled[:, :, :], q_scaled[:, :, :],
                                     w_row[:, :].unsqueeze(1).to_broadcast([P, AH, DH])).then_inc(pool_steps, 1)
                pool.wait_ge(pool_steps, at + 1)
                rotate(pool, nc, q_rotated[:, :, :], q_scaled[:, :, :], cos, sin, [w[:, :, :] for w in q_work],
                       pool_steps, at + 1, [P, AH, DH // 2])
                twice = q_rotated[:, :, :].unsqueeze(2).to_broadcast([P, AH, 2, DH])
                pool.wait_ge(pool_steps, at + 7)
                wait_for(pool, x_filled, fill(t - 1, 3))
                pass_waits(pool, pool_marks)
                for j in range(2):
                    nc.gpsimd.tensor_copy(q_twice[0][:, :, j, :].bitcast(F32R), q_rotated[:, :, :]).then_inc(pool_steps, 1)
                pool.wait_ge(pool_steps, at + 9)
                nc.gpsimd.tensor_sub(q_twice[1][:, :, :, :].bitcast(F32R), twice, q_twice[0][:, :, :, :]).then_inc(pool_steps, 1)

            def finish(t, g, count):
                n = 2 * t + g
                wait_for(pool, o_ready, n)
                pool.wait_ge(x_copied, count)
                nc.gpsimd.tensor_add(o_sum[:, :, :], o_parts[g][:, :, 0:DH], o_parts[g][:, :, DH:2 * DH]).then_inc(o_steps, 1)
                if g == 0:
                    wait_for(pool, stored, 16 * t)
                    wait_for(pool, squared, t)
                pool.wait_ge(inverted, n + 1)
                pool.wait_ge(o_steps, n + 1)
                cols = slice(g * GROUP * DH, (g + 1) * GROUP * DH)
                nc.gpsimd.tensor_mul(o_att[:, cols].rearrange("p (h c) -> p h c", c=DH), o_sum[:, :, :],
                                     inverse[g][:, :].unsqueeze(2).to_broadcast([P, GROUP, DH])).then_inc(o_ready, 1)

            def body(t, first, last):
                if not first:
                    finish(t - 1, 1, fill(t, 1))
                if not last:
                    prepare(t + 1)
                finish(t, 0, fill(t, 4))

            pool.wait_ge(w_here, 16)
            prepare(0)
            tiles(pool, body)
            finish(NT - 1, 1, fill(NT - 1, 5))

        @block.tensor
        def _(pe):
            def turn_queries(group, part):
                for h in range(GROUP):
                    last = nc.tensor.transpose(ps_x[:, h * P:(h + 1) * P],
                                               q_twice[part][:, group * GROUP + h, :, :].rearrange("p a c -> p (a c)"),
                                               const["ident"][:, :])
                last.then_inc(x_filled, 1)

            def turn_outputs(n):
                pe.wait_ge(o_copied, n + 1)
                for h in range(GROUP):
                    last = nc.tensor.transpose(ps_x[:, h * P:(h + 1) * P], o_turned[:, h * P:(h + 1) * P],
                                               const["ident"][:, :])
                last.then_inc(x_filled, 1)

            def score(head, h):
                for j in range(2):
                    cols = slice(j * BANK, (j + 1) * BANK)
                    keys = k_turned[:, head // GROUP, (2 * h + j) * BANK:(2 * h + j + 1) * BANK]
                    nc.tensor.matmul(ps_s[h][:, cols], q_turned[0][:, head, :], keys, start=True, stop=False)
                    last = nc.tensor.matmul(ps_s[h][:, cols], q_turned[1][:, head, :], keys, start=False, stop=True)
                last.then_inc(scored, 1)

            def body(t, first, last):
                if not first:
                    pe.wait_ge(x_copied, fill(t, 0))
                for u in range(AH):
                    U = t * AH + u
                    for h in range(2):
                        pe.wait_ge(exp_done, 2 * U + h + 1)
                        if not (last and u == AH - 1):
                            if h == 0 and u == 3:
                                pe.wait_ge(x_copied, fill(t, 3))
                            if h == 0 and u == AH - 1:
                                pe.wait_ge(x_copied, fill(t, 6))
                            score((u + 1) % AH, h)
                        for j in range(2 * h, 2 * h + 2):
                            wait_for(pe, lo_ready, 4 * U + j - 1)
                            for c in range(4):
                                ins = nc.tensor.transpose(ps_t[j % 2][:, c * P:(c + 1) * P],
                                                          probs[u % 2][:, (4 * j + c) * P:(4 * j + c + 1) * P],
                                                          const["ident"][:, :])
                            ins.then_inc(turned, 1)
                    if u % GROUP == GROUP - 1:
                        g = u // GROUP
                        wait_for(pe, o_copied, 2 * t + g)
                        pe.wait_ge(lo_ready, 4 * U + 4)
                        for c in range(NT):
                            for part in (probs_hi, probs_lo):
                                ins = nc.tensor.matmul(ps_o[:, :], v_split[:, c, g, :],
                                                       part[:, c, :, :].rearrange("p h q -> p (h q)"),
                                                       start=(c == 0 and part is probs_hi),
                                                       stop=(c == NT - 1 and part is probs_lo))
                        ins.then_inc(multiplied, 1)
                    if u == 0 and not first:
                        turn_outputs(2 * t - 1)
                    if u in (1, 2):
                        pe.wait_ge(x_copied, fill(t, u))
                        turn_queries(1, u - 1)
                    if u == 4:
                        pe.wait_ge(x_copied, fill(t, 3))
                        turn_outputs(2 * t)
                    if u in (5, 6) and not last:
                        pe.wait_ge(x_copied, fill(t, u - 1))
                        pe.wait_ge(pool_steps, 10 * (t + 2))
                        turn_queries(0, u - 5)

            pe.wait_ge(pool_steps, 10)
            turn_queries(0, 0)
            pe.wait_ge(x_copied, 1)
            turn_queries(0, 1)
            pe.wait_ge(x_copied, 2)
            score(0, 0)
            score(0, 1)
            body(0, True, False)
            with pe.Fori(1, NT - 1) as t:
                body(t, False, False)
            body(NT - 1, False, True)
            turn_outputs(2 * NT - 1)

        @block.scalar
        def _(act):
            def copy_queries(count, group, part):
                act.wait_ge(x_filled, count)
                nc.scalar.activation(q_turned[part][:, group * GROUP:(group + 1) * GROUP, :],
                                     ps_x[:, :].rearrange("p (h q) -> p h q", q=P), ACT.Copy).then_inc(x_copied, 1)

            def copy_outputs(count, g):
                act.wait_ge(x_filled, count)
                nc.scalar.activation(flat(o_parts[g]), ps_x[:, :], ACT.Copy).then_inc(x_copied, 1)

            def take_products(n):
                act.wait_ge(multiplied, n + 1)
                nc.scalar.activation(o_turned[:, :], ps_o[:, :], ACT.Copy).then_inc(o_copied, 1)

            def square(t):
                act.wait_ge(o_ready, 2 * t + 2)
                nc.scalar.activation(squares[:, :], o_att[:, :], ACT.Square,
                                     accum_out=att_squares[:, bass.ds(t, 1)]).then_inc(squared, 1)

            def exponentials(U, u):
                act.wait_ge(max_ready, U + 1)
                wait_for(act, turned, 4 * U - 4)
                for h in range(2):
                    nc.scalar.activation(probs[u % 2][:, h * L // 2:(h + 1) * L // 2], ps_s[h][:, :], ACT.Exp,
                                         bias=less_max[u % 2][:, :], scale=SCALE,
                                         accum_out=half_sums[u // GROUP][:, u % GROUP, h:h + 1]).then_inc(exp_done, 1)

            def body(t, first, last):
                for u in range(AH):
                    U = t * AH + u
                    if u == 0 and not first:
                        take_products(2 * t - 1)
                    if u == 1 and not first:
                        copy_outputs(fill(t, 1), 1)
                    if u in (2, 3):
                        copy_queries(fill(t, u), 1, u - 2)
                    if u == 3 and not first:
                        square(t - 1)
                    if u == 4:
                        take_products(2 * t)
                    if u == 5:
                        copy_outputs(fill(t, 4), 0)
                    if u in (6, 7) and not last:
                        copy_queries(fill(t, u - 1), 0, u - 6)
                    for j in range(4):
                        if j == 0 and u % GROUP == 0:
                            wait_for(act, multiplied, 2 * t + u // GROUP)
                        act.wait_ge(turned, 4 * U + j + 1)
                        nc.scalar.activation(probs_hi[:, 4 * j:4 * j + 4, u % GROUP, :],
                                             ps_t[j % 2][:, :].rearrange("p (c q) -> p c q", q=P),
                                             ACT.Copy).then_inc(hi_ready, 1)
                    if not (last and u == AH - 1):
                        exponentials(U + 1, (u + 1) % AH)

            for part in range(2):
                copy_queries(part + 1, 0, part)
            exponentials(0, 0)
            tiles(act, body)
            take_products(2 * NT - 1)
            copy_outputs(fill(NT - 1, 5), 1)
            square(NT - 1)

        @block.vector
        def _(dve):
            def half_maximum(U, s, h):
                dve.wait_ge(scored, 2 * U + h + 1)
                nc.vector.tensor_reduce(half_max[s][:, h:h + 1], ps_s[h][:, :], AX.X, ALU.max).then_inc(halved, 1)

            def maximum(U, s):
                dve.wait_ge(halved, 2 * U + 2)
                wait_for(dve, exp_done, 2 * U - 2)
                nc.vector.tensor_scalar(less_max[s][:, :], half_max[s][:, 0:1], half_max[s][:, 1:2], -SCALE,
                                        ALU.max, ALU.mult).then_inc(max_ready, 1)

            def remainder(U, u, j, t):
                dve.wait_ge(hi_ready, 4 * U + j + 1)
                cols = probs_hi[:, 4 * j:4 * j + 4, u % GROUP, :]
                nc.vector.tensor_sub(probs_lo[:, 4 * j:4 * j + 4, u % GROUP, :],
                                     ps_t[j % 2][:, :].rearrange("p (c q) -> p c q", q=P), f32(cols)).then_inc(lo_ready, 1)

            def invert(n, g):
                dve.wait_ge(exp_done, 2 * GROUP * (n + 1))
                nc.vector.tensor_reduce(sums[g][:, :], half_sums[g][:, :, :], AX.X, ALU.add).then_inc(summed, 1)
                dve.wait_ge(summed, n + 1)
                nc.vector.reciprocal(inverse[g][:, :], sums[g][:, :]).then_inc(inverted, 1)

            def body(t, first, last):
                for u in range(AH):
                    U, more = t * AH + u, not (last and u == AH - 1)
                    if u == 0 and not first:
                        invert(2 * t - 1, 1)
                    if u == 4:
                        invert(2 * t, 0)
                    if more:
                        half_maximum(U + 1, (u + 1) % 2, 0)
                    remainder(U, u, 0, t)
                    remainder(U, u, 1, t)
                    if more:
                        half_maximum(U + 1, (u + 1) % 2, 1)
                        maximum(U + 1, (u + 1) % 2)
                    remainder(U, u, 2, t)
                    remainder(U, u, 3, t)

            half_maximum(0, 0, 0)
            half_maximum(0, 0, 1)
            maximum(0, 0)
            tiles(dve, body)
            invert(2 * NT - 1, 1)


def project_output(nc, const, o_squares, att_squares, x2_squares, hg_norm_w, att_norm_w, w_out, x, tok_scr, mix_scr,
                   x2_scr):
    ctx, sems = ExitStack(), []
    with ctx:
        def sb(name, shape, dt=FP32):
            return ctx.enter_context(nc.sbuf_tensor(name, shape, dt))

        def pair(name, shape, dt=FP32):
            return [sb(f"{name}{s}", shape, dt) for s in range(2)]

        def sem(name):
            return stage_semaphore(nc, sems, name)

        raw = [sb(f"w_out_raw{k}", [P, D]) for k in range(2)]
        w_hi, w_lo = sb("w_out_hi", [P, KD, D], F32R), sb("w_out_lo", [P, KD, D], F32R)
        hg_row, att_row = sb("hg_norm_row", [P, P]), sb("att_norm_row", [P, AQW])
        o_root, o_rstd = sb("o_root", [P, NT, HG]), sb("o_rstd", [P, NT, HG])
        a_root, a_rstd = sb("att_root", [P, NT]), sb("att_rstd", [P, NT])
        mix, gate, x_res = pair("mix", [P, D]), pair("gate", [P, HGW]), pair("x_res", [P, D])
        gain, scaled, normed = pair("gain", [P, HGW]), pair("hg_scaled", [P, HGW]), pair("mix_normed", [P, D])
        m_hi, m_lo = pair("mixT_hi", [P, KD, P], F32R), pair("mixT_lo", [P, KD, P], F32R)
        x2, squares = pair("x2", [P, D]), sb("x2_sq", [P, D])
        ps_t = [ctx.enter_context(nc.psum_tensor(f"mix_ps_t{j}", [P, BANK], FP32)) for j in range(2)]
        ps_o = [[ctx.enter_context(nc.psum_tensor(f"x2_ps{s}{j}", [P, BANK], FP32)) for j in range(2)] for s in range(2)]
        w_here = [sem(f"w_out_here{s}") for s in range(2)]
        rows_here, rooted, rstds = sem("norm_rows_here"), sem("roots_ready"), sem("rstds_ready")
        w_hi_ready, w_ready = sem("w_out_hi_ready"), sem("w_out_ready")
        mix_here, gate_here, x_here = ([sem(f"{n}_here{s}") for s in range(2)] for n in ("mix", "gate", "x_res"))
        gained, normed_ready = sem("gate_and_scale_ready"), sem("mix_normed_ready")
        turned, hi_ready, lo_ready = sem("mix_turned"), sem("mixT_hi_ready"), sem("mixT_lo_ready")
        done, added, squared = sem("x2_product_done"), sem("x2_ready"), sem("x2_squared")
        stored = [sem(f"x2_stored{s}") for s in range(2)]
        ident = const["ident"]
        block = stage_block(nc, ctx, sems)

        def heads(t):
            return t.rearrange("p (h c) -> p h c", c=P)

        def steps(eng, step):
            step(0, 0)
            step(1, 1)
            with eng.Fori(1, NT // 2) as i:
                step(2 * i, 0)
                step(2 * i + 1, 1)

        @block.sync
        def _(sp):
            sp.dma_start(hg_row[:, :], hg_norm_w.partition_broadcast(P)).then_inc(rows_here, 16)
            sp.dma_start(att_row[:, :], att_norm_w.partition_broadcast(P)).then_inc(rows_here, 16)

            def load(t, s):
                rows = bass.ds(t * P, P)
                wait_for(sp, gained, 2 * t - 2)
                sp.dma_start(gate[s][:, :], tok_scr[rows, C_G:C_G + HGW]).then_inc(gate_here[s], 16)
                wait_for(sp, normed_ready, 2 * t - 2)
                sp.dma_start(mix[s][:, :], mix_scr[rows, :]).then_inc(mix_here[s], 16)

            def load_x(t, s):
                rows = bass.ds(t * P, P)
                wait_for(sp, added, t - 1)
                sp.dma_start(x_res[s][:, :], x[rows, :]).then_inc(x_here[s], 16)

            def store(t, s):
                sp.wait_ge(added, t + 1)
                sp.dma_start(x2_scr[bass.ds(t * P, P), :], x2[s][:, :]).then_inc(stored[s], 16)

            load(0, 0)
            load_x(0, 0)
            for k in range(KD):
                if k >= 2:
                    sp.wait_ge(w_ready, k - 1)
                sp.dma_start(raw[k % 2][:, :], w_out[k * P:(k + 1) * P, :]).then_inc(w_here[k % 2], 16)
            load(1, 1)
            load_x(1, 1)
            with sp.Fori(1, NT // 2) as i:
                for s in range(2):
                    load(2 * i + s, s)
                    load_x(2 * i + s, s)
                    store(2 * i + s - 2, s)
            store(NT - 2, 0)
            store(NT - 1, 1)
            for s in range(2):
                sp.wait_ge(stored[s], 8 * NT)

        @block.gpsimd
        def _(pool):
            def step(t, s):
                pool.wait_ge(gate_here[s], 8 * (t - s) + 16)
                wait_for(pool, normed_ready, 2 * t - 2)
                nc.gpsimd.tensor_mul(heads(gain[s][:, :]), heads(gate[s][:, :]),
                                     hg_row[:, :].unsqueeze(1).to_broadcast([P, HG, P])).then_inc(gained, 1)
                pool.wait_ge(mix_here[s], 8 * (t - s) + 16)
                rstd = o_rstd[:, bass.ds(t, 1), :].rearrange("p o h -> p (o h)")
                nc.gpsimd.tensor_mul(heads(scaled[s][:, :]), heads(mix[s][:, 0:HGW]),
                                     rstd.unsqueeze(2).to_broadcast([P, HG, P])).then_inc(gained, 1)

            pool.wait_ge(rows_here, 32)
            pool.wait_ge(rstds, 2)
            steps(pool, step)

        @block.scalar
        def _(act):
            nc.scalar.activation(o_root[:, :, :], o_squares[:, :, :], ACT.Sqrt, bias=const["eps"][:, :],
                                 scale=1.0 / P).then_inc(rooted, 1)
            nc.scalar.activation(a_root[:, :], att_squares[:, :], ACT.Sqrt, bias=const["eps"][:, :],
                                 scale=1.0 / AQW).then_inc(rooted, 1)

            def round_hi(t, s):
                wait_for(act, done, t - 1)
                for j in range(2):
                    act.wait_ge(turned, 2 * t + j + 1)
                    nc.scalar.activation(m_hi[s][:, 4 * j:4 * j + 4, :], ps_t[j][:, :].rearrange("p (k t) -> p k t", t=P),
                                         ACT.Copy).then_inc(hi_ready, 1)

            def square(t, s):
                wait_for(act, squared, t)
                act.wait_ge(added, t + 1)
                nc.scalar.activation(squares[:, :], x2[s][:, :], ACT.Square,
                                     accum_out=x2_squares[:, bass.ds(t, 1)]).then_inc(squared, 1)

            round_hi(0, 0)
            for k in range(KD):
                act.wait_ge(w_here[k % 2], 16 * (k // 2) + 16)
                nc.scalar.activation(w_hi[:, k, :], raw[k % 2][:, :], ACT.Copy).then_inc(w_hi_ready, 1)
            round_hi(1, 1)
            def tiles(i):
                for s in range(2):
                    round_hi(2 * i + s, s)
                    square(2 * i + s - 2, s)

            tiles(1)
            with act.Fori(2, NT // 2) as i:
                tiles(i)
            square(NT - 2, 0)
            square(NT - 1, 1)

        @block.vector
        def _(dve):
            dve.wait_ge(rooted, 2)
            nc.vector.reciprocal(o_rstd[:, :, :], o_root[:, :, :]).then_inc(rstds, 1)
            nc.vector.reciprocal(a_rstd[:, :], a_root[:, :]).then_inc(rstds, 1)

            def normalise(t, s):
                dve.wait_ge(mix_here[s], 8 * (t - s) + 16)
                wait_for(dve, turned, 2 * t - 2)
                nc.vector.scalar_tensor_tensor(out=normed[s][:, HGW:D], in0=mix[s][:, HGW:D],
                                               scalar=a_rstd[:, bass.ds(t, 1)], in1=att_row[:, :],
                                               op0=ALU.mult, op1=ALU.mult).then_inc(normed_ready, 1)
                dve.wait_ge(gained, 2 * t + 2)
                nc.vector.tensor_mul(normed[s][:, 0:HGW], gain[s][:, :], scaled[s][:, :]).then_inc(normed_ready, 1)

            def remainder(t, s):
                for j in range(2):
                    dve.wait_ge(hi_ready, 2 * t + j + 1)
                    nc.vector.tensor_sub(m_lo[s][:, 4 * j:4 * j + 4, :], ps_t[j][:, :].rearrange("p (k t) -> p k t", t=P),
                                         f32(m_hi[s][:, 4 * j:4 * j + 4, :])).then_inc(lo_ready, 1)

            def add(t, s):
                dve.wait_ge(done, t + 1)
                dve.wait_ge(x_here[s], 8 * (t - s) + 16)
                wait_for(dve, stored[s], 8 * (t - s))
                wait_for(dve, squared, t - 1)
                nc.vector.tensor_add(x2[s][:, 0:BANK], ps_o[s][0][:, :], x_res[s][:, 0:BANK])
                nc.vector.tensor_add(x2[s][:, BANK:D], ps_o[s][1][:, :], x_res[s][:, BANK:D]).then_inc(added, 1)

            dve.wait_ge(rows_here, 32)
            dve.wait_ge(rstds, 2)
            normalise(0, 0)
            remainder(0, 0)
            for k in range(KD):
                dve.wait_ge(w_hi_ready, k + 1)
                nc.vector.tensor_sub(w_lo[:, k, :], raw[k % 2][:, :], f32(w_hi[:, k, :])).then_inc(w_ready, 1)
            normalise(1, 1)
            remainder(1, 1)
            def tiles(i):
                for s in range(2):
                    normalise(2 * i + s, s)
                    add(2 * i + s - 2, s)
                    remainder(2 * i + s, s)

            tiles(1)
            with dve.Fori(2, NT // 2) as i:
                tiles(i)
            add(NT - 2, 0)
            add(NT - 1, 1)

        @block.tensor
        def _(pe):
            def turn(t, s):
                pe.wait_ge(normed_ready, 2 * t + 2)
                for j in range(2):
                    wait_for(pe, lo_ready, 2 * t + j - 1)
                    for k in range(4 * j, 4 * j + 4):
                        last = nc.tensor.transpose(ps_t[j][:, (k % 4) * P:(k % 4 + 1) * P],
                                                   normed[s][:, k * P:(k + 1) * P], ident[:, :])
                    last.then_inc(turned, 1)

            def multiply(t, s):
                pe.wait_ge(lo_ready, 2 * t + 2)
                wait_for(pe, added, t - 1)
                for j in range(2):
                    cols = slice(j * BANK, (j + 1) * BANK)
                    last = split_products(nc, ps_o[s][j][:, :], (lambda k: m_hi[s][:, k, :], lambda k: m_lo[s][:, k, :]),
                                          (lambda k: w_hi[:, k, cols], lambda k: w_lo[:, k, cols]), KD)
                last.then_inc(done, 1)

            turn(0, 0)
            turn(1, 1)
            pe.wait_ge(w_ready, KD)
            multiply(0, 0)
            def tiles(i):
                turn(2 * i, 0)
                multiply(2 * i - 1, 1)
                turn(2 * i + 1, 1)
                multiply(2 * i, 0)

            tiles(1)
            with pe.Fori(2, NT // 2) as i:
                tiles(i)
            multiply(NT - 1, 1)


def feed_forward(nc, const, half, x2_squares, w2_row, final_row, w_gate_up, w_down, x2_scr, out):
    NP = NF // 2
    TB = HALF // BANK
    YB = HT * D // BANK
    ctx, sems = ExitStack(), []
    with ctx:
        def sb(name, shape, dt=FP32):
            return ctx.enter_context(nc.sbuf_tensor(f"{name}_{half}", shape, dt))

        def pair(name, shape, dt=FP32):
            return [sb(f"{name}{s}", shape, dt) for s in range(2)]

        def pb(name, n):
            return [ctx.enter_context(nc.psum_tensor(f"{name}{j}_{half}", [P, BANK], FP32)) for j in range(n)]

        def sem(name):
            return stage_semaphore(nc, sems, f"{name}_{half}")

        y = sb("y", [P, HT, D])
        hT_hi, hT_lo = sb("h2T_hi", [P, KD, HALF], F32R), sb("h2T_lo", [P, KD, HALF], F32R)
        gu_raw, gu_hi, gu_lo = pair("gu_raw", [P, KD, 2, P]), pair("gu_hi", [P, KD, 2, P], F32R), pair("gu_lo", [P, KD, 2, P], F32R)
        d_raw, d_hi, d_lo = sb("d_raw", [P, 2, D]), sb("d_hi", [P, 2, D], F32R), sb("d_lo", [P, 2, D], F32R)
        silu, act_f = pair("silu", [P, BANK]), sb("act", [P, max(HALF, D)])
        act_hi, act_lo = pair("act_hi", [P, HALF], F32R), pair("act_lo", [P, HALF], F32R)
        h2 = [sb("h2", [P, D]), act_f]
        root, rstd = sb("x2_root", [P, HT]), sb("x2_rstd", [P, HT])
        y_total, y_root, y_rstd = sb("y_total", [P, HT]), sb("y_root", [P, HT]), sb("y_rstd", [P, HT])
        ps_g, ps_u, ps_y = pb("ps_g", TB), pb("ps_u", TB), pb("ps_y", 4)
        y_here, rooted, rstds = sem("y_here"), sem("x2_root_ready"), sem("x2_rstd_ready")
        h2_ready, turned, hi_ready, lo_ready = sem("h2_ready"), sem("h2_turned"), sem("h2T_hi_ready"), sem("h2T_lo_ready")
        gu_here, d_here = [sem(f"gu_here{s}") for s in range(2)], sem("d_here")
        gu_rounded, gu_ready, d_rounded, d_ready = sem("gu_hi_ready"), sem("gu_ready"), sem("d_hi_ready"), sem("d_ready")
        gated, silued, activated = sem("gate_up_done"), sem("silu_ready"), sem("act_ready")
        act_rounded, act_ready = sem("act_hi_ready"), sem("act_split")
        down_done, y_added = sem("down_done"), sem("y_added")
        y_squared, y_rooted, y_scale, out_ready = sem("y_squared"), sem("y_root_ready"), sem("y_rstd_ready"), sem("out_ready")
        stored = sem("out_stored")
        tile0 = half * HT
        rows = slice(half * HALF, (half + 1) * HALF)
        gu_cols = w_gate_up.rearrange("(k p) (a n) -> a p k n", p=P, a=2)
        d_rows = w_down.rearrange("(i a p) n -> i p a n", p=P, a=2)
        block = stage_block(nc, ctx, sems)

        @block.sync
        def _(sp):
            def load_gate_up(f, s):
                wait_for(sp, gu_ready, f - 1)
                for a in range(2):
                    sp.dma_start(gu_raw[s][:, :, a, :], gu_cols[a, :, :, bass.ds(f * P, P)]).then_inc(gu_here[s], 16)

            def load_down(i):
                wait_for(sp, d_ready, i)
                sp.dma_start(d_raw[:, :, :], d_rows[bass.ds(i, 1), :, :, :].rearrange("o p a n -> (o p) a n")).then_inc(d_here, 16)

            sp.dma_start(y[:, :, :], x2_scr[rows, :].rearrange("(t p) c -> p t c", p=P)).then_inc(y_here, 16)
            load_gate_up(0, 0)
            load_gate_up(1, 1)
            load_down(0)
            with sp.Fori(1, NP) as i:
                load_gate_up(2 * i, 0)
                load_gate_up(2 * i + 1, 1)
                load_down(i)
            for t in range(HT):
                sp.wait_ge(out_ready, t + 1)
                sp.dma_start(out[(tile0 + t) * P:(tile0 + t + 1) * P, :], y[:, t, :]).then_inc(stored, 16)
            sp.wait_ge(stored, 16 * HT)

        @block.gpsimd
        def _(pool):
            def split_gate_up(f, s):
                pool.wait_ge(gu_rounded, f + 1)
                nc.gpsimd.tensor_sub(gu_lo[s][:, :, :, :], gu_raw[s][:, :, :, :], f32(gu_hi[s][:, :, :, :])).then_inc(gu_ready, 1)

            def split_down(i):
                pool.wait_ge(d_rounded, i + 1)
                nc.gpsimd.tensor_sub(d_lo[:, :, :], d_raw[:, :, :], f32(d_hi[:, :, :])).then_inc(d_ready, 1)

            split_gate_up(0, 0)
            split_gate_up(1, 1)
            with pool.Fori(0, NP - 1) as i:
                split_gate_up(2 * i + 2, 0)
                split_down(i)
                split_gate_up(2 * i + 3, 1)
            split_down(NP - 1)

        @block.scalar
        def _(act):
            def round_gate_up(f, s):
                act.wait_ge(gu_here[s], 16 * (f - s) + 32)
                wait_for(act, gated, 2 * TB * (f - 1))
                nc.scalar.activation(gu_hi[s][:, :, :, :], gu_raw[s][:, :, :, :], ACT.Copy).then_inc(gu_rounded, 1)

            def round_down(i):
                act.wait_ge(d_here, 16 * i + 16)
                wait_for(act, down_done, YB * i)
                nc.scalar.activation(d_hi[:, :, :], d_raw[:, :, :], ACT.Copy).then_inc(d_rounded, 1)

            def silus(f):
                for tb in range(TB):
                    act.wait_ge(gated, 2 * TB * f + 2 * tb + 1)
                    wait_for(act, activated, TB * f + tb - 1)
                    nc.scalar.activation(silu[tb][:, :], ps_g[tb][:, :], ACT.Silu).then_inc(silued, 1)

            def round_act(f, s, i):
                wait_for(act, down_done, YB * i)
                for tb in range(TB):
                    cols = slice(tb * BANK, (tb + 1) * BANK)
                    act.wait_ge(activated, TB * f + tb + 1)
                    nc.scalar.activation(act_hi[s][:, cols], act_f[:, cols], ACT.Copy).then_inc(act_rounded, 1)

            nc.scalar.activation(root[:, :], x2_squares[:, tile0:tile0 + HT], ACT.Sqrt, bias=const["eps"][:, :],
                                 scale=1.0 / D).then_inc(rooted, 1)
            round_gate_up(0, 0)
            round_gate_up(1, 1)
            for t in range(HT):
                for j in range(2):
                    act.wait_ge(turned, 2 * t + j + 1)
                    nc.scalar.activation(hT_hi[:, 4 * j:4 * j + 4, t * P:(t + 1) * P],
                                         ps_y[2 * (t % 2) + j][:, :].rearrange("p (k t) -> p k t", t=P),
                                         ACT.Copy).then_inc(hi_ready, 1)

            def body(i, more):
                silus(2 * i)
                if more:
                    round_gate_up(2 * i + 2, 0)
                round_act(2 * i, 0, i)
                round_down(i)
                silus(2 * i + 1)
                round_act(2 * i + 1, 1, i)
                if more:
                    round_gate_up(2 * i + 3, 1)

            body(0, True)
            with act.Fori(1, NP - 1) as i:
                body(i, True)
            body(NP - 1, False)
            for t in range(HT):
                wait_for(act, y_squared, t - 1)
                act.wait_ge(y_added, YB * (NP - 1) + 2 * t + 2)
                nc.scalar.activation(h2[t % 2][:, :], y[:, t, :], ACT.Square, accum_out=y_total[:, t:t + 1]).then_inc(y_squared, 1)
            act.wait_ge(y_squared, HT)
            nc.scalar.activation(y_root[:, :], y_total[:, :], ACT.Sqrt, bias=const["eps"][:, :],
                                 scale=1.0 / D).then_inc(y_rooted, 1)

        @block.vector
        def _(dve):
            dve.wait_ge(rooted, 1)
            nc.vector.reciprocal(rstd[:, :], root[:, :]).then_inc(rstds, 1)
            dve.wait_ge(y_here, 16)
            dve.wait_ge(rstds, 1)
            for t in range(HT + 1):
                if t < HT:
                    if t >= 2:
                        dve.wait_ge(turned, 2 * t - 2)
                    nc.vector.scalar_tensor_tensor(out=h2[t % 2][:, :], in0=y[:, t, :], scalar=rstd[:, t:t + 1],
                                                   in1=w2_row[:, :], op0=ALU.mult, op1=ALU.mult).then_inc(h2_ready, 1)
                if t >= 1:
                    for j in range(2):
                        cols = (slice(None), slice(4 * j, 4 * j + 4), slice((t - 1) * P, t * P))
                        dve.wait_ge(hi_ready, 2 * t - 1 + j)
                        nc.vector.tensor_sub(hT_lo[cols], ps_y[2 * ((t - 1) % 2) + j][:, :].rearrange("p (k t) -> p k t", t=P),
                                             f32(hT_hi[cols])).then_inc(lo_ready, 1)

            def activate(f):
                for tb in range(TB):
                    dve.wait_ge(silued, TB * f + tb + 1)
                    dve.wait_ge(gated, 2 * TB * f + 2 * tb + 2)
                    wait_for(dve, act_rounded, TB * (f - 1) + tb + 1)
                    wait_for(dve, act_ready, TB * (f - 1) + tb + 1)
                    nc.vector.tensor_mul(act_f[:, tb * BANK:(tb + 1) * BANK], silu[tb][:, :], ps_u[tb][:, :]).then_inc(activated, 1)

            def remainder(f, s):
                for tb in range(TB):
                    cols = slice(tb * BANK, (tb + 1) * BANK)
                    dve.wait_ge(act_rounded, TB * f + tb + 1)
                    nc.vector.tensor_sub(act_lo[s][:, cols], act_f[:, cols], f32(act_hi[s][:, cols])).then_inc(act_ready, 1)

            def add(i):
                for n in range(YB):
                    t, cols = n // 2, slice((n % 2) * BANK, (n % 2 + 1) * BANK)
                    dve.wait_ge(down_done, YB * i + n + 1)
                    wait_for(dve, y_added, YB * (i - 1) + n + 1)
                    nc.vector.tensor_add(y[:, t, cols], ps_y[n % 4][:, :], y[:, t, cols]).then_inc(y_added, 1)

            def body(i, first):
                activate(2 * i)
                if not first:
                    add(i - 1)
                remainder(2 * i, 0)
                activate(2 * i + 1)
                remainder(2 * i + 1, 1)

            body(0, True)
            body(1, False)
            with dve.Fori(2, NP) as i:
                body(i, False)
            add(NP - 1)
            dve.wait_ge(y_rooted, 1)
            nc.vector.reciprocal(y_rstd[:, :], y_root[:, :]).then_inc(y_scale, 1)
            dve.wait_ge(y_scale, 1)
            for t in range(HT):
                nc.vector.scalar_tensor_tensor(out=y[:, t, :], in0=y[:, t, :], scalar=y_rstd[:, t:t + 1],
                                               in1=final_row[:, :], op0=ALU.mult, op1=ALU.mult).then_inc(out_ready, 1)

        @block.tensor
        def _(pe):
            for t in range(HT):
                pe.wait_ge(h2_ready, t + 1)
                for j in range(2):
                    if t >= 2:
                        pe.wait_ge(lo_ready, 2 * t + j - 3)
                    for k in range(4 * j, 4 * j + 4):
                        last = nc.tensor.transpose(ps_y[2 * (t % 2) + j][:, (k % 4) * P:(k % 4 + 1) * P],
                                                   h2[t % 2][:, k * P:(k + 1) * P], const["ident"][:, :])
                    last.then_inc(turned, 1)

            def gate_up(f, s):
                pe.wait_ge(gu_ready, f + 1)
                for tb in range(TB):
                    cols = slice(tb * BANK, (tb + 1) * BANK)
                    for a, ps in ((0, ps_g), (1, ps_u)):
                        wait_for(pe, activated, TB * (f - 1) + tb + 1)
                        split_products(nc, ps[tb][:, :], (lambda k: gu_hi[s][:, k, a, :], lambda k: gu_lo[s][:, k, a, :]),
                                       (lambda k: hT_hi[:, k, cols], lambda k: hT_lo[:, k, cols]), KD).then_inc(gated, 1)

            def down(i):
                pe.wait_ge(d_ready, i + 1)
                pe.wait_ge(act_ready, 2 * TB * (i + 1))
                for n in range(YB):
                    t, cols = n // 2, slice((n % 2) * BANK, (n % 2 + 1) * BANK)
                    toks = slice(t * P, (t + 1) * P)
                    wait_for(pe, y_added, YB * i + n - 3)
                    split_products(nc, ps_y[n % 4][:, :], (lambda a: act_hi[a][:, toks], lambda a: act_lo[a][:, toks]),
                                   (lambda a: d_hi[:, a, cols], lambda a: d_lo[:, a, cols]), 2).then_inc(down_done, 1)

            pe.wait_ge(lo_ready, 2 * HT)
            def pair_of_tiles(i):
                gate_up(2 * i, 0)
                down(i - 1)
                gate_up(2 * i + 1, 1)

            gate_up(0, 0)
            gate_up(1, 1)
            pair_of_tiles(1)
            with pe.Fori(2, NP) as i:
                pair_of_tiles(i)
            down(NP - 1)


def load_rows(nc, rows):
    ctx, sems = ExitStack(), []
    with ctx:
        rows_here = stage_semaphore(nc, sems, "final_rows_here")
        block = stage_block(nc, ctx, sems)

        @block.sync
        def _(sp):
            for tile, weights in rows:
                sp.dma_start(tile[:, :], weights.partition_broadcast(P)).then_inc(rows_here, 16)
            sp.wait_ge(rows_here, 16 * len(rows))


def encoder_layer(nc, out, x, norm1_w, w_in, lb_logits, hg_norm_w, q_norm_w, k_norm_w, att_norm_w, w_out, norm2_w,
                  w_gate_up, w_down, final_norm_w, rope):
    ctx = ExitStack()
    with ctx:
        def sb(name, shape, dt=FP32):
            return ctx.enter_context(nc.sbuf_tensor(name, shape, dt))

        def scratch(name, shape):
            return nc.dram_tensor(name, shape, FP32, kind="Internal").ap()

        q_scr, f_scr, k_scr = scratch("q_scr", (HG, P, L)), scratch("f_scr", (2 * HG, P, L)), scratch("k_scr", (2 * HG, P, L))
        tok_scr, mix_scr, x2_scr = scratch("tok_scr", (L, TOKEN_COLS)), scratch("mix_scr", (L, D)), scratch("x2_scr", (L, D))
        const = {"ident": sb("ident", [P, P]), "eps": sb("eps", [P, 1])}
        head_squares, head_rstd = sb("head_squares", [P, NT, NS]), sb("head_rstd", [P, NT, NS])
        o_squares, att_squares, x2_squares = sb("o_squares", [P, NT, HG]), sb("att_squares", [P, NT]), sb("x2_squares", [P, NT])
        with nc.sbuf_tensor("hT_hi", [P, KD, L], F32R) as hT_hi, nc.sbuf_tensor("hT_lo", [P, KD, L], F32R) as hT_lo:
            normalise_input(nc, const, hT_hi, hT_lo, x[0], norm1_w[0])
            project_input(nc, head_squares, hT_hi, hT_lo, w_in[0], lb_logits, q_scr, f_scr, k_scr, tok_scr)
        with nc.sbuf_tensor("o_back", [P, NT, HGW], FP32) as o_back:
            for forward in (False, True):
                recurrence(nc, const, forward, o_back, o_squares, q_scr, f_scr, k_scr, tok_scr, mix_scr)
        with nc.sbuf_tensor("k_turned", [P, KVH, L], F32R) as k_turned, \
                nc.sbuf_tensor("v_split", [P, NT, KVH, 2 * DH], F32R) as v_split, \
                nc.sbuf_tensor("rope_sb", [P, 2, NT, DH // 2], FP32) as rope_sb:
            prepare_keys(nc, const, head_squares, head_rstd, rope_sb, k_turned, v_split, k_norm_w[0], rope, tok_scr)
            attention(nc, const, head_rstd, rope_sb, k_turned, v_split, att_squares, q_norm_w[0], tok_scr, mix_scr)
        project_output(nc, const, o_squares, att_squares, x2_squares, hg_norm_w[0], att_norm_w[0], w_out[0], x[0],
                       tok_scr, mix_scr, x2_scr)
        w2_row, final_row = sb("norm2_row", [P, D]), sb("final_row", [P, D])
        load_rows(nc, [(w2_row, norm2_w[0]), (final_row, final_norm_w)])
        for half in range(2):
            feed_forward(nc, const, half, x2_squares, w2_row, final_row, w_gate_up[0], w_down[0], x2_scr, out[0])


_INS = ["x", "norm1_w", "w_in", "lb_logits", "hg_norm_w", "q_norm_w", "k_norm_w", "att_norm_w", "w_out", "norm2_w",
        "w_gate_up", "w_down", "final_norm_w"]


def kernel(**inputs):
    import numpy as _np
    import concourse.bacc as _bacc
    from concourse import mybir as _mybir
    from concourse.bass_utils import run_bass_kernel_spmd as _run

    nc = _bacc.Bacc("TRN2", target_bir_lowering=False, num_devices=1)
    arrays = {f"in_{n}_dram": _np.ascontiguousarray(inputs[n]) for n in _INS}
    grid_w, pairs = 64, 32
    freqs = _np.float32(10000.0) ** (-_np.arange(0, 32, 2, dtype=_np.float32) / _np.float32(32))
    token = _np.arange(2048)
    angle = _np.concatenate([(token // grid_w).astype(_np.float32)[:, None] * freqs,
                             (token % grid_w).astype(_np.float32)[:, None] * freqs], axis=-1).astype(_np.float32)
    arrays["in_rope_dram"] = _np.stack([_np.cos(angle), _np.sin(angle)]).astype(_np.float32).reshape(2, 2048, pairs)
    args = {}
    for name in _INS + ["rope"]:
        a = arrays[f"in_{name}_dram"]
        args[name] = nc.dram_tensor(f"in_{name}_dram", a.shape, _mybir.dt.from_np(a.dtype), kind="ExternalInput").ap()
    out = nc.dram_tensor("out_0_dram", (1, 2048, 1024), _mybir.dt.float32, kind="ExternalOutput").ap()
    encoder_layer(nc, out=out, **args)
    r = _run(nc, [arrays], core_ids=[0])
    return r.results[0]["out_0_dram"]
```

```python
import concourse.bass as bass
from concourse import mybir
from contextlib import ExitStack

FP32 = mybir.dt.float32
F32R = mybir.dt.float32r
ACT = mybir.ActivationFunctionType
ALU = mybir.AluOpType
AX = mybir.AxisListType

P = 128
L = 2048
D = 1024
KD = D // P
NT = L // P
BANK = 512
EPS = 1e-6

HG = 4
HGW = HG * P
CHUNK = 64
CPT = P // CHUNK
AH, KVH, DH = 8, 2, 64
GROUP = AH // KVH
AQW, AKW = AH * DH, KVH * DH
NS = AH + KVH

WB = 256
FEATURE_COLS = 3 * HGW
TOKEN_COLS = 2 * HGW + AQW + 2 * AKW
C_I, C_G, C_AQ, C_AK = 0, HGW, 2 * HGW, 2 * HGW + AQW

DFF = 2816
NF = DFF // P
HALF = L // 2
HT = HALF // P
SPLIT = 3


def f32(ap):
    return ap.bitcast(FP32)


def stage_semaphore(nc, sems, name):
    sems.append(nc.alloc_semaphore(name=name))
    return sems[-1]


def stage_block(nc, ctx, sems):
    def clear():
        nc.clear_and_free_semaphores(sems)
        nc.all_engine_barrier()

    ctx.callback(clear)
    return ctx.enter_context(nc.Block())


def split_products(nc, out, stationary, moving, steps, part=None):
    (s_hi, s_lo), (m_hi, m_lo) = stationary, moving
    for k in part or range(steps):
        nc.tensor.matmul(out, s_hi(k), m_hi(k), start=(k == 0), stop=False)
        nc.tensor.matmul(out, s_hi(k), m_lo(k), start=False, stop=False)
        last = nc.tensor.matmul(out, s_lo(k), m_hi(k), start=False, stop=(k == steps - 1))
    return last


def load_columns(rows):
    return rows.rearrange("(k p) n -> p k n", p=P)


def project_input(nc, const, head_squares, hT_hi, hT_lo, x, norm1_w, w_in, lb_logits, q_scr, f_scr, k_scr, tok_scr):
    FB = FEATURE_COLS // WB
    NB = (FEATURE_COLS + TOKEN_COLS) // WB
    TB = L // BANK
    FU = 2 * TB
    ctx, sems = ExitStack(), []
    with ctx:
        def sb(name, shape, dt=FP32):
            return ctx.enter_context(nc.sbuf_tensor(name, shape, dt))

        def sem(name):
            return stage_semaphore(nc, sems, name)

        raw = [sb(f"w_raw{s}", [P, KD, WB]) for s in range(2)]
        w_hi = [sb(f"w_hi{s}", [P, KD, WB], F32R) for s in range(2)]
        w_lo = [sb(f"w_lo{s}", [P, KD, WB], F32R) for s in range(2)]
        sig_negative = sb("sig_negative", [P, 2 * BANK])
        sig = [[sb(f"sig{s}", [P, BANK]), sig_negative[:, s * BANK:(s + 1) * BANK]] for s in range(2)]
        stage = [[sb(f"stage{s}{j}", [P, 2 * BANK]) for j in range(2)] for s in range(2)]
        logits, lb_exp = sb("lb_logits_sb", [P, 2, 2, HG]), sb("lb_exp", [P, 2, 2, HG])
        lb_work = sb("lb_work", [P, 3, 2, HG])
        lb, one_less = sb("lb", [P, 2 * HG]), sb("one_less_lb", [P, 2 * HG])
        x_tile, squares = [stage[s][1] for s in range(2)], sig_negative
        h_tile = [raw[1][:, s * KD // 2:(s + 1) * KD // 2, :].rearrange("p k n -> p (k n)") for s in range(2)]
        w_row = sb("norm1_row", [P, D])
        total, root, rstd = ([sb(f"x_{name}{s}", [P, 1]) for s in range(2)] for name in ("total", "root", "rstd"))
        ident, eps = const["ident"], const["eps"]
        ps = [ctx.enter_context(nc.psum_tensor(f"u_ps{b}", [P, BANK], FP32)) for b in range(8)]
        w_arrived = [sem(f"w_arrived{s}") for s in range(2)]
        w_hi_ready, w_split, w_slot_free = sem("w_hi_ready"), sem("w_split"), sem("w_slot_free")
        u_done, act_done, u_out = sem("u_done"), sem("u_act_done"), sem("u_out")
        stored = [sem(f"stored{s}") for s in range(2)]
        k_stored = [sem(f"k_stored{s}") for s in range(2)]
        x_in, w_row_in = [sem(f"x_in{s}") for s in range(2)], sem("norm1_in")
        const_ready, zeroed = sem("const_ready"), sem("ident_zeroed")
        total_ready, root_ready, rstd_ready = sem("x_total_ready"), sem("x_root_ready"), sem("x_rstd_ready")
        h_ready, h_turned, hi_ready, lo_ready = sem("h_ready"), sem("h_turned"), sem("hT_hi_ready"), sem("hT_lo_ready")
        half_turned = sem("h_half_turned")
        lb_in, lb_step, lb_exped = sem("lb_in"), sem("lb_step"), sem("lb_exped")
        w_cols = load_columns(w_in)
        tok_rows = tok_scr.rearrange("(g t p) c -> g p t c", t=4, p=P)
        block = stage_block(nc, ctx, sems)

        turned = [ps[4:6], ps[6:8]]

        def first_units(t):
            units = [(t // 4 - 1) * 2 + t % 4 // 2] if t >= 4 and t % 2 else []
            return units + ([FU - 2, FU - 1] if t == NT - 1 else [])

        def token_part(ap, t):
            return ap[:, :, t * P:(t + 1) * P]

        def unit0(b):
            return b * FU if isinstance(b, int) and b < FB else FB * FU + (b - FB) * NT

        @block.sync
        def _(sp):
            def load(b, s):
                sp.dma_start(raw[s][:, :, :], w_cols[:, :, bass.ds(b * WB, WB)]).then_inc(w_arrived[s], 16)

            def load_after_split(b, s):
                sp.wait_ge(w_split, b - 1)
                load(b, s)

            def store_feature(b, with_k):
                for g in range(4):
                    f, half, s = g // 2, g % 2, g % 2
                    tile = 2 * b + f
                    cols = slice(half * 2 * BANK, (half + 1) * 2 * BANK)
                    sp.wait_ge(u_out, b * FU + 2 * g + 2)
                    if not with_k:
                        sp.dma_start(q_scr[tile, :, cols], stage[s][0][:, :]).then_inc(stored[s], 16)
                    else:
                        sp.dma_start(f_scr[bass.ds(tile - HG, 1), :, cols].rearrange("o p t -> (o p) t"),
                                     stage[s][0][:, :]).then_inc(stored[s], 16)
                        sp.dma_start(k_scr[bass.ds(tile - HG, 1), :, cols].rearrange("o p t -> (o p) t"),
                                     stage[s][1][:, :]).then_inc(k_stored[s], 16)

            def store_token(b):
                for g in range(4):
                    sp.wait_ge(u_out, unit0(b) + 4 * g + 4)
                    sp.dma_start(tok_rows[g, :, :, (b - FB) * WB:(b - FB + 1) * WB],
                                 stage[g % 2][0][:, :].rearrange("p (t c) -> p t c", t=4)).then_inc(stored[g % 2], 16)

            sp.dma_start(w_row[:, :], norm1_w.partition_broadcast(P)).then_inc(w_row_in, 16)
            for t in range(NT):
                if t >= 2:
                    sp.wait_ge(h_ready, t - 1)
                sp.dma_start(x_tile[t % 2][:, :], x[t * P:(t + 1) * P, :]).then_inc(x_in[t % 2], 16)
                if t == 1:
                    load(0, 0)
            def store_first(half):
                for f in range(2):
                    sp.wait_ge(u_out, 4 * half + 3 + f)
                    sp.dma_start(q_scr[f, :, half * 2 * BANK:(half + 1) * 2 * BANK], stage[f][0][:, :]).then_inc(stored[f], 16)

            store_first(0)
            sp.wait_ge(h_turned, NT)
            load(1, 1)
            for j in range(2):
                for d in range(2):
                    sp.dma_start(logits[:, d, j, :], lb_logits[d, j, :].rearrange("(h p) -> p h", p=P),
                                 allow_slow_non_contiguous=True).then_inc(lb_in, 16)
            load_after_split(2, 0)
            store_first(1)
            load_after_split(3, 1)
            store_feature(1, False)
            with sp.Fori(1, FB // 2) as i:
                for s in range(2):
                    load_after_split(2 * i + s + 2, s)
                    store_feature(2 * i + s, True)
            for b in range(FB, NB):
                if b + 2 < NB:
                    load_after_split(b + 2, b % 2)
                store_token(b)
            for s in range(2):
                sp.wait_ge(stored[s], 16 * 2 * NB)
                sp.wait_ge(k_stored[s], 16 * 2 * (FB - 2))

        @block.gpsimd
        def _(pool):
            def split(b, s, used):
                pool.wait_ge(w_arrived[s], 16 + 8 * (b - s))
                if used is not None:
                    pool.wait_ge(u_done, used)
                pool.sem_inc(w_slot_free, 1)
                nc.gpsimd.tensor_copy(w_hi[s][:, :, :], raw[s][:, :, :]).then_inc(w_hi_ready, 1)
                pool.wait_ge(w_hi_ready, b + 1)
                nc.gpsimd.tensor_sub(w_lo[s][:, :, :], raw[s][:, :, :], f32(w_hi[s][:, :, :])).then_inc(w_split, 1)

            nc.gpsimd.memset(ident[:, :], 0.0).then_inc(zeroed, 1)
            nc.gpsimd.memset(eps[:, :], EPS).then_inc(const_ready, 1)
            pool.wait_ge(zeroed, 1)
            nc.gpsimd.affine_select(out=ident[:, :], in_=ident[:, :], compare_op=ALU.not_equal, fill=1.0, base=0,
                                    pattern=[[-1, P]], channel_multiplier=1).then_inc(const_ready, 1)
            split(0, 0, None)
            split(1, 1, None)
            with pool.Fori(1, FB // 2 + 1) as i:
                split(2 * i, 0, (2 * i - 1) * FU)
                split(2 * i + 1, 1, 2 * i * FU)
            for b in range(FB + 2, NB):
                split(b, b % 2, unit0(b - 1))

        @block.tensor
        def _(pe):
            def feature_block(b, s):
                pe.wait_ge(w_split, b + 1)
                for f in range(2):
                    for tb in range(TB):
                        n = TB * f + tb
                        pe.wait_ge(u_out, min(n + 5, FU) if isinstance(b, int) else b * FU + n - 7)
                        cols = slice(tb * BANK, (tb + 1) * BANK)
                        split_products(
                            nc, ps[TB * f + tb][:, :],
                            (lambda k: w_hi[s][:, k, f * P:(f + 1) * P], lambda k: w_lo[s][:, k, f * P:(f + 1) * P]),
                            (lambda k: hT_hi[:, k, cols], lambda k: hT_lo[:, k, cols]), KD).then_inc(u_done, 1)

            def token_block(b, s):
                pe.wait_ge(w_split, b + 1)
                for t in range(NT):
                    pe.wait_ge(u_out, b * NT - FB * (NT - FU) + t - 7)
                    toks = slice(t * P, (t + 1) * P)
                    split_products(
                        nc, ps[t % 8][:, 0:WB],
                        (lambda k: hT_hi[:, k, toks], lambda k: hT_lo[:, k, toks]),
                        (lambda k: w_hi[s][:, k, :], lambda k: w_lo[s][:, k, :]), KD).then_inc(u_done, 1)

            def turn(t):
                pe.wait_ge(h_ready, t + 1)
                for j in range(2):
                    if t >= 2:
                        pe.wait_ge(lo_ready, 2 * t - 3 + j)
                    for k in range(4 * j, 4 * j + 4):
                        last = nc.tensor.transpose(turned[t % 2][j][:, (k % 4) * P:(k % 4 + 1) * P],
                                                   h_tile[t % 2][:, k * P:(k + 1) * P], ident[:, :])
                    if j == 0:
                        last.then_inc(half_turned, 1)
                last.then_inc(h_turned, 1)

            pe.wait_ge(const_ready, 2)
            for t in range(4):
                turn(t)
            pe.wait_ge(w_split, 1)
            for n in range(FU):
                tb, f = n // 2, n % 2
                cols = slice(tb * BANK, (tb + 1) * BANK)
                pe.wait_ge(lo_ready, 8 * (tb + 1))
                if n >= 4:
                    pe.wait_ge(u_out, n - 3)
                for half in range(2):
                    last = split_products(
                        nc, ps[n % 4][:, :],
                        (lambda k: w_hi[0][:, k, f * P:(f + 1) * P], lambda k: w_lo[0][:, k, f * P:(f + 1) * P]),
                        (lambda k: hT_hi[:, k, cols], lambda k: hT_lo[:, k, cols]), KD,
                        range(half * KD // 2, (half + 1) * KD // 2))
                    if half == 1:
                        last.then_inc(u_done, 1)
                    if tb < TB - 1:
                        turn(4 * tb + 4 + 2 * f + half)
            feature_block(1, 1)
            with pe.Fori(1, FB // 2) as i:
                feature_block(2 * i, 0)
                feature_block(2 * i + 1, 1)
            with pe.Fori(FB // 2, NB // 2) as i:
                token_block(2 * i, 0)
                token_block(2 * i + 1, 1)
            token_block(NB - 1, (NB - 1) % 2)

        @block.scalar
        def _(act):
            def feature_units(b, both):
                for n in range(FU):
                    act.wait_ge(u_done, b * FU + n + 1)
                    act.wait_ge(u_out, b * FU + n - 1)
                    ins = nc.scalar.activation(sig[n % 2][0][:, :], ps[n][:, :], ACT.Sigmoid)
                    if both:
                        ins = nc.scalar.activation(sig[n % 2][1][:, :], ps[n][:, :], ACT.Sigmoid, scale=-1.0)
                    ins.then_inc(act_done, 1)

            def token_units(b, func):
                for t in range(NT):
                    n = unit0(b) + t
                    act.wait_ge(u_done, n + 1)
                    act.wait_ge(u_out, n - 1)
                    nc.scalar.activation(sig[t % 2][0][:, 0:WB], ps[t % 8][:, 0:WB], func).then_inc(act_done, 1)

            def statistics(t):
                s = t % 2
                act.wait_ge(x_in[s], 16 * (t // 2) + 16)
                nc.scalar.activation(squares[:, :], x_tile[s][:, :], ACT.Square,
                                     accum_out=total[s][:, :]).then_inc(total_ready, 1)
                act.wait_ge(total_ready, t + 1)
                nc.scalar.activation(root[s][:, :], total[s][:, :], ACT.Sqrt, bias=eps[:, :],
                                     scale=1.0 / D).then_inc(root_ready, 1)

            act.wait_ge(const_ready, 2)
            statistics(0)
            for t in range(NT):
                if t + 1 < NT:
                    statistics(t + 1)
                for j in range(2):
                    if j == 0:
                        act.wait_ge(half_turned, t + 1)
                    else:
                        act.wait_ge(h_turned, t + 1)
                    nc.scalar.activation(token_part(hT_hi[:, 4 * j:4 * j + 4, :], t),
                                         turned[t % 2][j][:, :].rearrange("p (k t) -> p k t", t=P), ACT.Copy).then_inc(hi_ready, 1)
                for n in first_units(t):
                    act.wait_ge(u_done, n + 1)
                    if n >= 2:
                        act.wait_ge(u_out, n - 1)
                    nc.scalar.activation(sig[n % 2][0][:, :], ps[n % 4][:, :], ACT.Sigmoid).then_inc(act_done, 1)
            act.wait_ge(lb_step, 2)
            nc.scalar.activation(lb_exp[:, :, :, :], logits[:, :, :, :], ACT.Exp).then_inc(lb_exped, 1)
            feature_units(1, False)
            with act.Fori(1, FB // 2) as i:
                feature_units(2 * i, True)
                feature_units(2 * i + 1, True)
            for b in range(FB + 2, FB + 4):
                token_units(b, ACT.Sigmoid)
            for b in range(FB + 4, NB):
                token_units(b, ACT.Square)

        @block.vector
        def _(dve):
            def scale(t):
                s = t % 2
                dve.wait_ge(root_ready, t + 1)
                nc.vector.reciprocal(rstd[s][:, :], root[s][:, :]).then_inc(rstd_ready, 1)
                if t >= 2:
                    dve.wait_ge(h_turned, t - 1)
                dve.wait_ge(rstd_ready, t + 1)
                nc.vector.scalar_tensor_tensor(out=h_tile[s], in0=x_tile[s][:, :], scalar=rstd[s][:, :],
                                               in1=w_row[:, :], op0=ALU.mult, op1=ALU.mult).then_inc(h_ready, 1)

            dve.wait_ge(w_row_in, 16)
            scale(0)
            for t in range(NT):
                if t + 1 < NT:
                    scale(t + 1)
                for j in range(2):
                    dve.wait_ge(hi_ready, 2 * t + 1 + j)
                    nc.vector.tensor_sub(token_part(hT_lo[:, 4 * j:4 * j + 4, :], t),
                                         turned[t % 2][j][:, :].rearrange("p (k t) -> p k t", t=P),
                                         f32(token_part(hT_hi[:, 4 * j:4 * j + 4, :], t))).then_inc(lo_ready, 1)
                for n in first_units(t):
                    f, half, cols = n % 2, n // 4, slice((n // 2 % 2) * BANK, (n // 2 % 2 + 1) * BANK)
                    dve.wait_ge(act_done, n + 1)
                    if half == 1 and n // 2 % 2 == 0:
                        dve.wait_ge(stored[f], 16)
                    nc.vector.tensor_mul(stage[f][0][:, cols], ps[n % 4][:, :], sig[f][0][:, :]).then_inc(u_out, 1)

            l0, l1 = logits[:, :, 0, :], logits[:, :, 1, :]
            top, total, inverse = (lb_work[:, j, :, :] for j in range(3))
            dve.wait_ge(lb_in, 64)
            nc.vector.tensor_max(top, l0, l1).then_inc(lb_step, 1)
            dve.wait_ge(lb_step, 1)
            nc.vector.tensor_sub(l0, l0, top)
            nc.vector.tensor_sub(l1, l1, top).then_inc(lb_step, 1)
            dve.wait_ge(lb_exped, 1)
            nc.vector.tensor_add(total, lb_exp[:, :, 0, :], lb_exp[:, :, 1, :]).then_inc(lb_step, 1)
            dve.wait_ge(lb_step, 3)
            nc.vector.reciprocal(inverse, total).then_inc(lb_step, 1)
            dve.wait_ge(lb_step, 4)
            nc.vector.tensor_mul(lb[:, :].rearrange("p (d h) -> p d h", h=HG), lb_exp[:, :, 0, :],
                                 inverse).then_inc(lb_step, 1)
            dve.wait_ge(lb_step, 5)
            nc.vector.tensor_scalar(one_less[:, :], lb[:, :], -1.0, 1.0, ALU.mult, ALU.add).then_inc(lb_step, 1)
            dve.wait_ge(lb_step, 6)

            def feature_units(b, gates):
                for n in range(FU):
                    g, tile = n // 2, 2 * b + n // TB
                    s, cols = g % 2, slice((n % 2) * BANK, (n % 2 + 1) * BANK)
                    dve.wait_ge(act_done, b * FU + n + 1)
                    if n % 2 == 0:
                        dve.wait_ge(stored[s], 32 * b + 16 * (g // 2))
                    if not gates:
                        nc.vector.tensor_mul(stage[s][0][:, cols], ps[n][:, :], sig[n % 2][0][:, :]).then_inc(u_out, 1)
                    else:
                        col = bass.ds(tile - HG, 1)
                        nc.vector.tensor_scalar(stage[s][0][:, cols], sig[n % 2][0][:, :], one_less[:, col], lb[:, col],
                                                ALU.mult, ALU.add)
                        if n % 2 == 0:
                            dve.wait_ge(k_stored[s], 32 * (b - 2) + 16 * (g // 2) + 16)
                        nc.vector.tensor_scalar(stage[s][1][:, cols], sig[n % 2][1][:, :], one_less[:, col], None,
                                                ALU.mult).then_inc(u_out, 1)

            def token_units(b, kind, heads):
                for t in range(NT):
                    g = t // 4
                    s, cols = g % 2, slice((t % 4) * WB, (t % 4 + 1) * WB)
                    if kind == "copy":
                        dve.wait_ge(u_done, unit0(b) + t + 1)
                    else:
                        dve.wait_ge(act_done, unit0(b) + t + 1 - 2 * NT)
                    if t % 4 == 0:
                        dve.wait_ge(stored[s], 32 * b + 16 * (g // 2))
                    out = stage[s][0][:, cols]
                    if kind == "copy":
                        nc.vector.tensor_copy(out, ps[t % 8][:, 0:WB]).then_inc(u_out, 1)
                    elif kind == "silu":
                        nc.vector.tensor_mul(out, ps[t % 8][:, 0:WB], sig[t % 2][0][:, 0:WB]).then_inc(u_out, 1)
                    else:
                        n = (heads.stop - heads.start)
                        nc.vector.tensor_copy(out, ps[t % 8][:, 0:WB])
                        nc.vector.tensor_reduce(head_squares[:, t, heads],
                                                sig[t % 2][0][:, 0:n * DH].rearrange("p (h c) -> p h c", c=DH),
                                                AX.X, ALU.add).then_inc(u_out, 1)

            for s in range(2):
                dve.sem_inc(k_stored[s], 16)
            feature_units(1, False)
            with dve.Fori(1, FB // 2) as i:
                feature_units(2 * i, True)
                feature_units(2 * i + 1, True)
            for b, kind, heads in [(0, "copy", None), (1, "copy", None), (2, "silu", None), (3, "silu", None),
                                   (4, "squares", slice(0, 4)), (5, "squares", slice(4, 8)),
                                   (6, "squares", slice(8, 10))]:
                token_units(FB + b, kind, heads)


def wait_for(eng, sem, value):
    if not isinstance(value, int) or value > 0:
        eng.wait_ge(sem, value)


def pass_waits(eng, steps):
    eng.sem_inc(steps, 1)


def flat(t):
    return t[:, :, :].rearrange("p h t -> p (h t)")


def recurrence(nc, const, forward, o_back, o_squares, q_scr, f_scr, k_scr, tok_scr, mix_scr):
    way = "forward" if forward else "back"
    ctx, sems = ExitStack(), []
    with ctx:
        def sb(name, shape, dt=FP32):
            return [ctx.enter_context(nc.sbuf_tensor(f"{way}_{name}{s}", shape, dt)) for s in range(2)]

        def pb(name, n):
            return [ctx.enter_context(nc.psum_tensor(f"{way}_{name}{s}", [P, BANK], FP32)) for s in range(n)]

        def sem(name):
            return stage_semaphore(nc, sems, f"{way}_{name}")

        q, f, k = sb("r_q", [P, HG, P]), sb("r_f", [P, HG, P]), sb("r_k", [P, HG, P])
        v = sb("r_v", [P, HGW])
        log_f, b, b_mid, b_end = (sb(x, [P, HG * P]) for x in ("log_f", "b", "b_mid", "b_end"))
        e_in, e_key, e_out, e_b = (sb(x, [P, HG * P]) for x in ("e_in", "e_key", "e_out", "e_b"))
        q_in, k_in, k_out, q_out = (sb(x, [P, HG, P]) for x in ("q_inner", "k_inner", "k_outer", "q_outer"))
        k_turned = sb("k_turned", [P, HG, P])
        scores = sb("scores", [P, HG, CHUNK])
        o_tile, squares = sb("o_tile", [P, HGW]), sb("o_sq", [P, HGW])
        state = [ctx.enter_context(nc.sbuf_tensor(f"{way}_state{m}", [P, HG, P], FP32)) for m in range(2 * CPT)]
        keep = ctx.enter_context(nc.sbuf_tensor(f"{way}_keep", [P, HG, CHUNK], mybir.dt.int32))
        restart = ctx.enter_context(nc.sbuf_tensor(f"{way}_restart", [P, HG * P], FP32))
        ps_turn, ps_scores, ps_add, ps_o = pb("ps_turn", 1), pb("ps_scores", 1), pb("ps_add", 2), pb("ps_o", 2)
        q_here, f_here, k_here, v_here = ([sem(f"{x}_here{s}") for s in range(2)] for x in "qfkv")
        logs, cums, exps = sem("log_f_ready"), sem("cumulative_ready"), sem("exponentials_ready")
        q_in_ready, q_out_ready, k_ready = sem("q_in_ready"), sem("q_out_ready"), sem("k_in_out_ready")
        turned, turned_copied = sem("k_turned_psum"), sem("k_turned_ready")
        scored, masked = sem("scores_done"), sem("scores_masked")
        added, state_ready = sem("state_addend_done"), sem("state_ready")
        o_done, o_out = sem("o_done"), sem("o_out")
        o_stored = [sem(f"o_stored{s}") for s in range(2)]
        squared, prepared, zeroed = sem("o_squared"), sem("constants_ready"), sem("constants_zeroed")
        sp_steps, dve_steps = sem("sp_steps"), sem("dve_steps")
        order = (0, 1) if forward else (1, 0)
        mid, end = (CHUNK // 2 - 1, CHUNK - 1) if forward else (CHUNK // 2, 0)
        d = 0 if forward else 1
        block = stage_block(nc, ctx, sems)

        def first_token(n):
            return n * P if forward else L - P - n * P

        def in_order(ap):
            return ap if forward else ap[:, ::-1]

        def chunks(ap):
            return ap.rearrange("p (c t) -> p c t", t=CHUNK)

        def at_chunk(ap, t):
            return chunks(ap)[:, :, t:t + 1].to_broadcast([P, HG * CPT, CHUNK])

        def iterations(eng, core, scoring, gates):
            def iteration(n, s):
                if not isinstance(n, int) or 1 <= n:
                    core(n - 1, 1 - s)
                if not isinstance(n, int) or n < NT:
                    scoring(n, s)
                if not isinstance(n, int) or n + 1 < NT:
                    gates(n + 1, 1 - s)

            gates(0, 0)
            for n in range(3):
                iteration(n, n % 2)
            with eng.Fori(0, (NT - 4) // 2) as i:
                iteration(2 * i + 3, 1)
                iteration(2 * i + 4, 0)
            iteration(NT - 1, 1)
            iteration(NT, 0)

        @block.sync
        def _(sp):
            def load(tile, here, scr, n, s, used, value):
                wait_for(sp, used, value)
                pass_waits(sp, sp_steps)
                sp.dma_start(tile[s][:, :, :], scr.rearrange("h p t -> p h t")[:, :, bass.ds(first_token(n), P)]).then_inc(here[s], 16)

            def load_f(n, s):
                load(f, f_here, f_scr[d * HG:(d + 1) * HG], n, s, logs, n - 1)

            def load_others(n, s):
                load(q, q_here, q_scr, n, s, q_out_ready, n - 1)
                load(k, k_here, k_scr[d * HG:(d + 1) * HG], n, s, k_ready, 2 * n - 2)
                wait_for(sp, o_done, n - 1)
                pass_waits(sp, sp_steps)
                sp.dma_start(v[s][:, :], tok_scr[bass.ds(first_token(n), P), C_I:C_I + HGW]).then_inc(v_here[s], 16)

            def store(n, s):
                rows = bass.ds(first_token(n), P)
                sp.wait_ge(o_out, n + 1)
                sp.dma_start(mix_scr[rows, 0:HGW], o_tile[s][:, :]).then_inc(o_stored[s], 16)

            def step(n, s):
                if not isinstance(n, int) or n + 1 < NT:
                    load_f(n + 1, 1 - s)
                load_others(n, s)
                if forward and (not isinstance(n, int) or n >= 2):
                    store(n - 2, s)

            load_f(0, 0)
            step(0, 0)
            step(1, 1)
            with sp.Fori(1, NT // 2 - 1) as i:
                for s in range(2):
                    step(2 * i + s, s)
            step(NT - 2, 0)
            step(NT - 1, 1)
            if forward:
                for n in range(NT - 2, NT):
                    store(n, n % 2)
                for s in range(2):
                    sp.wait_ge(o_stored[s], 8 * NT)

        @block.gpsimd
        def _(pool):
            nc.gpsimd.memset(keep[:, :, :], 1).then_inc(zeroed, 1)
            nc.gpsimd.memset(restart[:, :], 1.0).then_inc(zeroed, 1)
            for s in range(2):
                nc.gpsimd.memset(scores[s][:, :, :], 0.0).then_inc(zeroed, 1)
            nc.gpsimd.memset(state[0][:, :, :], 0.0).then_inc(zeroed, 1)
            pool.wait_ge(zeroed, 5)
            nc.gpsimd.memset(chunks(restart[:, :])[:, :, 0:1], 0.0).then_inc(prepared, 1)
            for c in range(CPT):
                pool.wait_ge(prepared, 1 + c)
                half, sign = keep[c * CHUNK:(c + 1) * CHUNK, :, :], 1 if forward else -1
                nc.gpsimd.affine_select(out=half, in_=half, compare_op=ALU.is_ge, fill=0, base=0,
                                        pattern=[[0, HG], [sign, CHUNK]], channel_multiplier=-sign).then_inc(prepared, 1)

            def gates(n, s):
                pool.wait_ge(k_here[s], 8 * (n - s) + 16)
                pool.wait_ge(exps, 4 * n + 2)
                wait_for(pool, scored, n - 1)
                nc.gpsimd.tensor_mul(flat(k_in[s]), flat(k[s]), e_key[s][:, :]).then_inc(k_ready, 1)
                pool.wait_ge(exps, 4 * n + 3)
                wait_for(pool, turned, n - 1)
                nc.gpsimd.tensor_mul(flat(k_out[s]), flat(k[s]), e_out[s][:, :]).then_inc(k_ready, 1)

            iterations(pool, lambda n, s: None, lambda n, s: None, gates)

        @block.scalar
        def _(act):
            def square(n, s):
                if forward:
                    act.wait_ge(o_out, n + 1)
                    for h in range(HG):
                        ins = nc.scalar.activation(squares[s][:, h * P:(h + 1) * P], o_tile[s][:, h * P:(h + 1) * P],
                                                   ACT.Square, accum_out=o_squares[:, bass.ds(n, 1), h:h + 1])
                    ins.then_inc(squared, 1)

            def scoring(n, s):
                act.wait_ge(turned, n + 1)
                wait_for(act, added, 2 * n - 2)
                nc.scalar.activation(flat(k_turned[s]), ps_turn[0][:, :], ACT.Copy).then_inc(turned_copied, 1)

            def logarithm(n, s):
                act.wait_ge(f_here[s], 8 * (n - s) + 16)
                wait_for(act, cums, 3 * n - 5)
                nc.scalar.activation(log_f[s][:, :], flat(f[s]), ACT.Ln).then_inc(logs, 1)

            def exponentials(n, s):
                act.wait_ge(cums, 3 * n + 2)
                wait_for(act, q_in_ready, n - 1)
                wait_for(act, k_ready, 2 * n - 2)
                nc.scalar.activation(e_in[s][:, :], b_mid[s][:, :], ACT.Exp).then_inc(exps, 1)
                nc.scalar.activation(e_key[s][:, :], b_mid[s][:, :], ACT.Exp, scale=-1.0).then_inc(exps, 1)
                act.wait_ge(cums, 3 * n + 3)
                nc.scalar.activation(e_out[s][:, :], b_end[s][:, :], ACT.Exp).then_inc(exps, 1)
                wait_for(act, q_out_ready, n - 1)
                wait_for(act, state_ready, 2 * n - 2)
                nc.scalar.activation(e_b[s][:, :], b[s][:, :], ACT.Exp).then_inc(exps, 1)

            def iteration(n, s):
                every = not isinstance(n, int)
                if every or n + 1 < NT:
                    exponentials(n + 1, 1 - s)
                if every or n + 2 < NT:
                    logarithm(n + 2, s)
                if every or n < NT:
                    scoring(n, s)
                if every or n >= 1:
                    square(n - 1, 1 - s)

            nc.scalar.preload_act_table_set("natural_log_exp_and_others")
            logarithm(0, 0)
            exponentials(0, 0)
            logarithm(1, 1)
            for n in range(3):
                iteration(n, n % 2)
            with act.Fori(0, (NT - 6) // 2) as i:
                iteration(2 * i + 3, 1)
                iteration(2 * i + 4, 0)
            for n in range(NT - 3, NT + 1):
                iteration(n, n % 2)

        @block.vector
        def _(dve):
            def update_states(n, s):
                for c in range(CPT):
                    m, lo = 2 * s + c, order[c] * CHUNK
                    dve.wait_ge(added, 2 * n + c + 1)
                    wait_for(dve, state_ready, 2 * n + c)
                    wait_for(dve, o_done, n - 1 + c)
                    for h in range(HG):
                        col = h * P + lo + end
                        last = nc.vector.scalar_tensor_tensor(
                            out=state[(m + 1) % 4][:, h, :], in0=state[m][:, h, :], scalar=e_b[s][:, col:col + 1],
                            in1=ps_add[c][:, h * P:(h + 1) * P], op0=ALU.mult, op1=ALU.add)
                    last.then_inc(state_ready, 1)

            def take_output(n, s):
                dve.wait_ge(o_done, n + 1)
                pass_waits(dve, dve_steps)
                t = n if forward else NT - 1 - n
                back = o_back[:, bass.ds(t, 1), :].rearrange("p o c -> p (o c)")
                if forward:
                    wait_for(dve, o_stored[s], 8 * (n - s))
                    wait_for(dve, squared, n - 1)
                    nc.vector.tensor_add(o_tile[s][:, :], ps_o[s][:, :], back).then_inc(o_out, 1)
                else:
                    nc.vector.tensor_copy(back, ps_o[s][:, :]).then_inc(o_out, 1)

            def cumulate(n, s):
                dve.wait_ge(logs, n + 1)
                wait_for(dve, exps, 4 * n - 4)
                nc.vector.tensor_tensor_scan(in_order(b[s][:, :]), restart[:, :], in_order(log_f[s][:, :]), 0.0,
                                             ALU.mult, ALU.add).then_inc(cums, 1)
                dve.wait_ge(cums, 3 * n + 1)
                nc.vector.tensor_sub(chunks(b_mid[s][:, :]), chunks(b[s][:, :]), at_chunk(b[s][:, :], mid)).then_inc(cums, 1)
                nc.vector.tensor_sub(chunks(b_end[s][:, :]), at_chunk(b[s][:, :], end), chunks(b[s][:, :])).then_inc(cums, 1)

            def query_in(n, s):
                dve.wait_ge(q_here[s], 8 * (n - s) + 16)
                dve.wait_ge(exps, 4 * n + 1)
                wait_for(dve, scored, n - 1)
                nc.vector.tensor_mul(flat(q_in[s]), flat(q[s]), e_in[s][:, :]).then_inc(q_in_ready, 1)

            def query_out(n, s):
                dve.wait_ge(exps, 4 * n + 4)
                wait_for(dve, o_done, n - 1)
                nc.vector.tensor_mul(flat(q_out[s]), flat(q[s]), e_b[s][:, :]).then_inc(q_out_ready, 1)

            def mask(n, s):
                nc.vector.copy_predicated(scores[s][:, :, :], keep[:, :, :],
                                          ps_scores[0][:, 0:HG * CHUNK].rearrange("p (h t) -> p h t", t=CHUNK)).then_inc(masked, 1)

            def iteration(n, s):
                every = not isinstance(n, int)
                if every or n >= 1:
                    update_states(n - 1, 1 - s)
                if every or n + 1 < NT:
                    cumulate(n + 1, 1 - s)
                if every or n >= 1:
                    take_output(n - 1, 1 - s)
                if every or n + 1 < NT:
                    query_in(n + 1, 1 - s)
                if every or n < NT:
                    dve.wait_ge(scored, n + 1)
                    wait_for(dve, o_done, n - 1)
                if every or n + 1 < NT:
                    query_out(n + 1, 1 - s)
                if every or n < NT:
                    mask(n, s)

            dve.wait_ge(prepared, 1 + CPT)
            cumulate(0, 0)
            query_in(0, 0)
            query_out(0, 0)
            for n in range(3):
                iteration(n, n % 2)
            with dve.Fori(0, (NT - 4) // 2) as i:
                iteration(2 * i + 3, 1)
                iteration(2 * i + 4, 0)
            iteration(NT - 1, 1)
            iteration(NT, 0)

        @block.tensor
        def _(pe):
            def core(n, s):
                pe.wait_ge(v_here[s], 8 * (n - s) + 16)
                pe.wait_ge(turned_copied, n + 1)
                for c in range(CPT):
                    half = slice(order[c] * CHUNK, (order[c] + 1) * CHUNK)
                    wait_for(pe, state_ready, 2 * n - 1 + c)
                    for h in range(HG):
                        last = nc.tensor.matmul(ps_add[c][:, h * P:(h + 1) * P], k_turned[s][half, h, :],
                                                v[s][half, h * P:(h + 1) * P], start=True, stop=True)
                    last.then_inc(added, 1)
                pe.wait_ge(masked, n + 1)
                pe.wait_ge(q_out_ready, n + 1)
                wait_for(pe, o_out, n - 1)
                for c in range(CPT):
                    half = slice(order[c] * CHUNK, (order[c] + 1) * CHUNK)
                    wait_for(pe, state_ready, 2 * n + c)
                    for h in range(HG):
                        cols = slice(h * P, (h + 1) * P)
                        nc.tensor.matmul(ps_o[s][half, cols], q_out[s][:, h, half], state[2 * s + c][:, h, :],
                                         start=True, stop=False)
                        last = nc.tensor.matmul(ps_o[s][half, cols], scores[s][half, h, :], v[s][half, cols],
                                                start=False, stop=True)
                last.then_inc(o_done, 1)

            def scoring(n, s):
                pe.wait_ge(k_ready, 2 * n + 2)
                wait_for(pe, turned_copied, n)
                for h in range(HG):
                    last = nc.tensor.transpose(ps_turn[0][:, h * P:(h + 1) * P], k_out[s][:, h, :], const["ident"][:, :])
                last.then_inc(turned, 1)
                pe.wait_ge(q_in_ready, n + 1)
                wait_for(pe, masked, n)
                for c in range(CPT):
                    half = slice(c * CHUNK, (c + 1) * CHUNK)
                    for h in range(HG):
                        last = nc.tensor.matmul(ps_scores[0][half, h * CHUNK:(h + 1) * CHUNK], k_in[s][:, h, half],
                                                q_in[s][:, h, half], start=True, stop=True)
                last.then_inc(scored, 1)

            pe.wait_ge(prepared, 1 + CPT)
            iterations(pe, core, scoring, lambda n, s: None)


def rotate(eng, nc, out, src, cos, sin, work, steps, at, shape):
    even, odd = src[..., 0::2], src[..., 1::2]
    cos, sin = cos.to_broadcast(shape), sin.to_broadcast(shape)
    for w, a, b in ((0, even, cos), (1, odd, sin), (2, even, sin), (3, odd, cos)):
        eng.tensor_mul(work[w], a, b).then_inc(steps, 1)
    eng.wait_ge(steps, at + 2)
    eng.tensor_sub(out[..., 0::2], work[0], work[1]).then_inc(steps, 1)
    eng.wait_ge(steps, at + 4)
    eng.tensor_add(out[..., 1::2], work[2], work[3]).then_inc(steps, 1)
    return at + 6


def prepare_keys(nc, const, head_squares, head_rstd, rope_sb, k_turned, v_split, k_norm_w, rope, tok_scr):
    ctx, sems = ExitStack(), []
    with ctx:
        def sb(name, shape, dt=FP32):
            return ctx.enter_context(nc.sbuf_tensor(name, shape, dt))

        def sem(name):
            return stage_semaphore(nc, sems, name)

        HALVES = 2
        keys, values = sb("keys", [P, NT, KVH, DH]), sb("values", [P, NT, KVH, DH])
        scaled, rotated = sb("k_scaled", [P, NT, KVH, DH]), sb("k_rotated", [P, NT, KVH, DH])
        work = [sb(f"k_work{w}", [P, NT, KVH, DH // 2]) for w in range(4)]
        k_split = sb("k_split", [P, NT, KVH, 2, DH])
        w_row, root = sb("k_norm_row", [P, DH]), sb("head_root", [P, NT, NS])
        ps = [ctx.enter_context(nc.psum_tensor(f"k_ps{b}", [P, BANK], FP32)) for b in range(8)]
        keys_in, loaded, v_in = sem("keys_in"), sem("k_norm_and_rope_in"), sem("v_in")
        rooted, steps = sem("head_root_ready"), sem("k_steps")
        v_hi_ready, turned, copied = sem("v_hi_ready"), sem("k_turned_done"), sem("k_copied")
        block = stage_block(nc, ctx, sems)
        rows = tok_scr.rearrange("(t p) c -> p t c", p=P)

        @block.sync
        def _(sp):
            sp.dma_start(keys[:, :, :, :].rearrange("p t h c -> p t (h c)"), rows[:, :, C_AK:C_AK + AKW]).then_inc(keys_in, 16)
            sp.dma_start(w_row[:, :], k_norm_w.partition_broadcast(P)).then_inc(loaded, 16)
            for j in range(2):
                sp.dma_start(rope_sb[:, j, :, :], rope[j].rearrange("(t p) c -> p t c", p=P)).then_inc(loaded, 16)
            sp.dma_start(values[:, :, :, :].rearrange("p t h c -> p t (h c)"),
                         rows[:, :, C_AK + AKW:TOKEN_COLS]).then_inc(v_in, 16)

        @block.scalar
        def _(act):
            nc.scalar.activation(root[:, :, :], head_squares[:, :, :], ACT.Sqrt, bias=const["eps"][:, :],
                                 scale=1.0 / DH).then_inc(rooted, 1)
            for b in range(8):
                act.wait_ge(turned, b + 1)
                t0 = 4 * (b % 4)
                nc.scalar.activation(k_turned[:, b // 4, t0 * P:(t0 + 4) * P], ps[b][:, :], ACT.Copy).then_inc(copied, 1)

        @block.gpsimd
        def _(pool):
            pool.wait_ge(v_in, 16)
            nc.gpsimd.tensor_copy(v_split[:, :, :, 0:DH], values[:, :, :, :]).then_inc(v_hi_ready, 1)
            pool.wait_ge(v_hi_ready, 1)
            nc.gpsimd.tensor_sub(v_split[:, :, :, DH:2 * DH], values[:, :, :, :], f32(v_split[:, :, :, 0:DH]))

        @block.vector
        def _(dve):
            dve.wait_ge(rooted, 1)
            nc.vector.reciprocal(head_rstd[:, :, :], root[:, :, :]).then_inc(steps, 1)
            dve.wait_ge(keys_in, 16)
            dve.wait_ge(steps, 1)
            nc.vector.tensor_mul(scaled[:, :, :, :], keys[:, :, :, :],
                                 head_rstd[:, :, AH:NS].unsqueeze(3).to_broadcast([P, NT, KVH, DH])).then_inc(steps, 1)
            dve.wait_ge(steps, 2)
            dve.wait_ge(loaded, 48)
            flat_heads = scaled[:, :, :, :].rearrange("p t h c -> p (t h) c")
            nc.vector.tensor_mul(flat_heads, flat_heads,
                                 w_row[:, :].unsqueeze(1).to_broadcast([P, NT * KVH, DH])).then_inc(steps, 1)
            dve.wait_ge(steps, 3)
            at = rotate(dve, nc, rotated[:, :, :, :], scaled[:, :, :, :], rope_sb[:, 0, :, :].unsqueeze(2),
                        rope_sb[:, 1, :, :].unsqueeze(2), [w[:, :, :, :] for w in work], steps, 3,
                        [P, NT, KVH, DH // 2])
            dve.wait_ge(steps, at)
            for h in range(KVH):
                nc.vector.tensor_copy(k_split[:, :, h, 0, :].bitcast(F32R), rotated[:, :, h, :]).then_inc(steps, 1)
            for h in range(KVH):
                dve.wait_ge(steps, at + 1 + h)
                nc.vector.tensor_sub(k_split[:, :, h, 1, :].bitcast(F32R), rotated[:, :, h, :],
                                     k_split[:, :, h, 0, :]).then_inc(steps, 1)

        @block.tensor
        def _(pe):
            for b in range(8):
                if b % 4 == 0:
                    pe.wait_ge(steps, 12 + b // 4)
                for t in range(4):
                    last = nc.tensor.transpose(ps[b][:, t * P:(t + 1) * P],
                                               k_split[:, 4 * (b % 4) + t, b // 4, :, :].rearrange("p a c -> p (a c)"),
                                               const["ident"][:, :])
                last.then_inc(turned, 1)


def attention(nc, const, head_rstd, rope_sb, k_turned, v_split, att_squares, q_norm_w, tok_scr, mix_scr):
    ctx, sems = ExitStack(), []
    with ctx:
        def sb(name, shape, dt=FP32):
            return ctx.enter_context(nc.sbuf_tensor(name, shape, dt))

        def pb(name, banks=1):
            return ctx.enter_context(nc.psum_tensor(name, [P, banks * BANK], FP32))

        def sem(name):
            return stage_semaphore(nc, sems, name)

        NG = AH // GROUP
        SCALE = float(DH) ** -0.5
        w_row = sb("q_norm_row", [P, DH])
        q_raw, q_scaled = sb("q_raw", [P, AH, DH]), sb("q_scaled", [P, AH, DH])
        q_rotated = sb("q_rotated", [P, AH, DH])
        q_work = [sb(f"q_work{w}", [P, AH, DH // 2]) for w in range(4)]
        q_twice = [sb(f"q_twice_{x}", [P, AH, 2, DH]) for x in ("hi", "lo")]
        q_turned = [sb(f"q_turned_{x}", [P, AH, P], F32R) for x in ("hi", "lo")]
        probs = [sb(f"probs{s}", [P, L]) for s in range(4)]
        probs_hi, probs_lo = ([sb(f"probs_{x}{s}", [P, NT, 2, P], F32R) for s in range(2)] for x in ("hi", "lo"))
        half_max = [sb(f"half_max{s}", [P, 2]) for s in range(2)]
        less_max = [sb(f"less_max{s}", [P, 1]) for s in range(2)]
        half_sums = [sb(f"half_sums{g}", [P, GROUP, 2]) for g in range(NG)]
        sums, inverse = [sb(f"sums{g}", [P, GROUP]) for g in range(NG)], [sb(f"inverse{g}", [P, GROUP]) for g in range(NG)]
        o_turned = [sb(f"att_o_turned{g}", [P, GROUP * P]) for g in range(NG)]
        o_parts = [sb(f"o_parts{g}", [P, GROUP, 2 * DH]) for g in range(NG)]
        o_sum, o_att, squares = sb("o_sum", [P, GROUP, DH]), sb("o_att", [P, AQW]), sb("att_sq", [P, AQW])
        ps_s = [pb(f"ps_s{h}", 2) for h in range(2)]
        ps_t, ps_o, ps_x = [pb(f"ps_t{b}") for b in range(2)], pb("ps_pv"), pb("ps_x")
        w_here, q_here, q_used, q_steps, pool_marks = (sem(x) for x in (
            "q_norm_here", "q_here", "q_used", "q_steps", "pool_marks"))
        scored, halved, max_ready, exp_done = (sem(x) for x in ("att_scored", "half_max_done", "less_max_ready", "exp_done"))
        turned, hi_ready, lo_ready = sem("probs_turned"), sem("probs_hi_ready"), sem("probs_lo_ready")
        multiplied, o_copied = sem("pv_done"), sem("o_copied")
        x_filled, x_copied = sem("x_filled"), sem("x_copied")
        summed, inverted = sem("sums_ready"), sem("inverse_ready")
        o_steps, o_ready, squared, stored = sem("o_sum_ready"), sem("o_att_ready"), sem("att_squared"), sem("att_stored")
        block = stage_block(nc, ctx, sems)

        def fill(t, j, first=False):
            return 6 * t + j + (2 if first and j <= 2 else 0)

        def tiles(eng, body, peeled=1):
            for t in range(peeled):
                body(t, t == 0, False)
            with eng.Fori(peeled, NT - 1) as t:
                body(t, False, False)
            body(NT - 1, False, True)

        STEPS = 10

        def prepare(eng, t, turned_before):
            at = t * STEPS
            rstd = head_rstd[:, bass.ds(t, 1), 0:AH].rearrange("p o h -> p (o h)")
            cos, sin = (rope_sb[:, j, bass.ds(t, 1), :] for j in range(2))
            eng.wait_ge(q_here, 16 * t + 16)
            eng.tensor_mul(q_scaled[:, :, :], q_raw[:, :, :], rstd.unsqueeze(2).to_broadcast([P, AH, DH])).then_inc(q_used, 1)
            eng.wait_ge(q_used, t + 1)
            eng.tensor_mul(q_scaled[:, :, :], q_scaled[:, :, :],
                           w_row[:, :].unsqueeze(1).to_broadcast([P, AH, DH])).then_inc(q_steps, 1)
            eng.wait_ge(q_steps, at + 1)
            rotate(eng, nc, q_rotated[:, :, :], q_scaled[:, :, :], cos, sin, [w[:, :, :] for w in q_work],
                   q_steps, at + 1, [P, AH, DH // 2])
            twice = q_rotated[:, :, :].unsqueeze(2).to_broadcast([P, AH, 2, DH])
            eng.wait_ge(q_steps, at + 7)
            wait_for(eng, x_filled, turned_before)
            if not isinstance(t, int) or t > 0:
                pass_waits(eng, pool_marks)
            for j in range(2):
                eng.tensor_copy(q_twice[0][:, :, j, :].bitcast(F32R), q_rotated[:, :, :]).then_inc(q_steps, 1)
            eng.wait_ge(q_steps, at + 9)
            eng.tensor_sub(q_twice[1][:, :, :, :].bitcast(F32R), twice, q_twice[0][:, :, :, :]).then_inc(q_steps, 1)

        @block.sync
        def _(sp):
            sp.dma_start(w_row[:, :], q_norm_w.partition_broadcast(P)).then_inc(w_here, 16)
            sp.dma_start(flat(q_raw), tok_scr[0:P, C_AQ:C_AQ + AQW]).then_inc(q_here, 16)

            def body(t, first, last):
                if not last:
                    sp.wait_ge(q_used, t + 1)
                    sp.dma_start(flat(q_raw), tok_scr[bass.ds(t * P + P, P), C_AQ:C_AQ + AQW]).then_inc(q_here, 16)
                if not first:
                    sp.wait_ge(o_ready, 2 * t)
                    sp.dma_start(mix_scr[bass.ds(t * P - P, P), HGW:D], o_att[:, :]).then_inc(stored, 16)

            tiles(sp, body)
            sp.wait_ge(o_ready, 2 * NT)
            sp.dma_start(mix_scr[L - P:L, HGW:D], o_att[:, :]).then_inc(stored, 16)
            sp.wait_ge(stored, 16 * NT)

        @block.gpsimd
        def _(pool):
            def finish(t, g, count):
                n = 2 * t + g
                wait_for(pool, o_ready, n)
                pool.wait_ge(x_copied, count)
                nc.gpsimd.tensor_add(o_sum[:, :, :], o_parts[g][:, :, 0:DH], o_parts[g][:, :, DH:2 * DH]).then_inc(o_steps, 1)
                if g == 0:
                    wait_for(pool, stored, 16 * t)
                    wait_for(pool, squared, t)
                pool.wait_ge(inverted, n + 1)
                pool.wait_ge(o_steps, n + 1)
                cols = slice(g * GROUP * DH, (g + 1) * GROUP * DH)
                nc.gpsimd.tensor_mul(o_att[:, cols].rearrange("p (h c) -> p h c", c=DH), o_sum[:, :, :],
                                     inverse[g][:, :].unsqueeze(2).to_broadcast([P, GROUP, DH])).then_inc(o_ready, 1)

            def body(t, first, last):
                if not last:
                    prepare(pool, t + 1, fill(t, 2, first))
                if not first:
                    finish(t - 1, 0, fill(t, 3))
                    finish(t - 1, 1, fill(t, 4))

            pool.wait_ge(q_steps, STEPS)
            tiles(pool, body, 2)
            finish(NT - 1, 0, fill(NT - 1, 5))
            finish(NT - 1, 1, fill(NT - 1, 6))

        @block.tensor
        def _(pe):
            def turn_queries(group, part):
                for h in range(GROUP):
                    last = nc.tensor.transpose(ps_x[:, h * P:(h + 1) * P],
                                               q_twice[part][:, group * GROUP + h, :, :].rearrange("p a c -> p (a c)"),
                                               const["ident"][:, :])
                last.then_inc(x_filled, 1)

            def turn_outputs(n, g):
                pe.wait_ge(o_copied, 2 * n + 2)
                for h in range(GROUP):
                    last = nc.tensor.transpose(ps_x[:, h * P:(h + 1) * P], o_turned[g][:, h * P:(h + 1) * P],
                                               const["ident"][:, :])
                last.then_inc(x_filled, 1)

            def score(head, h):
                for j in range(2):
                    cols = slice(j * BANK, (j + 1) * BANK)
                    keys = k_turned[:, head // GROUP, (2 * h + j) * BANK:(2 * h + j + 1) * BANK]
                    nc.tensor.matmul(ps_s[h][:, cols], q_turned[0][:, head, :], keys, start=True, stop=False)
                    last = nc.tensor.matmul(ps_s[h][:, cols], q_turned[1][:, head, :], keys, start=False, stop=True)
                last.then_inc(scored, 1)

            def turn(U, u, j):
                pe.wait_ge(exp_done, 2 * U + j // 2 + 1)
                wait_for(pe, lo_ready, 4 * U + j - 1)
                for c in range(4):
                    ins = nc.tensor.transpose(ps_t[j % 2][:, c * P:(c + 1) * P],
                                              probs[u % 4][:, (4 * j + c) * P:(4 * j + c + 1) * P], const["ident"][:, :])
                ins.then_inc(turned, 1)

            def multiply(p, j, part):
                if part == 0:
                    wait_for(pe, o_copied, p)
                pe.wait_ge(lo_ready, 8 * p + 5 + part)
                cols = slice((j % 2) * 2 * P, (j % 2 + 1) * 2 * P)
                for c in range(4 * part, 4 * part + 4):
                    for split in (probs_hi, probs_lo):
                        ins = nc.tensor.matmul(ps_o[:, cols], v_split[:, c, 2 * j // GROUP, :],
                                               split[j % 2][:, c, :, :].rearrange("p h q -> p (h q)"),
                                               start=(c == 0 and split is probs_hi),
                                               stop=(c == NT - 1 and split is probs_lo))
                if part == 3:
                    ins.then_inc(multiplied, 1)

            def body(t, first, last):
                for u in range(AH):
                    U = t * AH + u
                    more = not (last and u == AH - 1)
                    turning = not (first and u == 0)
                    behind = u // 2 - 1 if u % 2 else u // 2 - 2
                    parts = (0, 1) if u % 2 else (2, 3)
                    pair = (4 * t + behind, behind % 4)
                    multiplying = not (first and behind < 0)
                    if more:
                        if u == 3:
                            pe.wait_ge(x_copied, fill(t, 2, first))
                        if u == AH - 1:
                            pe.wait_ge(x_copied, fill(t, 6))
                        pe.wait_ge(exp_done, 2 * U + 1)
                        score((u + 1) % AH, 0)
                    if turning:
                        turn(U - 1, (u - 1) % AH, 0)
                        turn(U - 1, (u - 1) % AH, 1)
                    if more:
                        pe.wait_ge(exp_done, 2 * U + 2)
                        score((u + 1) % AH, 1)
                    if multiplying:
                        multiply(*pair, parts[0])
                    if turning:
                        turn(U - 1, (u - 1) % AH, 2)
                    if multiplying:
                        multiply(*pair, parts[1])
                    if turning:
                        turn(U - 1, (u - 1) % AH, 3)
                    if u in (0, 1):
                        pe.wait_ge(x_copied, fill(t, u, first))
                        turn_queries(1, u)
                    if u in (2, 3) and not first:
                        pe.wait_ge(x_copied, fill(t, u))
                        turn_outputs(2 * t + u - 4, u - 2)
                    if u in (4, 5) and not last:
                        pe.wait_ge(x_copied, fill(t, u))
                        pe.wait_ge(q_steps, STEPS * (t + 2))
                        turn_queries(0, u - 4)

            pe.wait_ge(q_steps, STEPS)
            turn_queries(0, 0)
            pe.wait_ge(x_copied, 1)
            turn_queries(0, 1)
            pe.wait_ge(x_copied, 2)
            score(0, 0)
            score(0, 1)
            tiles(pe, body)
            UNITS, PAIRS = AH * NT, AH * NT // 2
            for j in range(4):
                turn(UNITS - 1, AH - 1, j)
            for part in (2, 3):
                multiply(PAIRS - 2, 2, part)
            pe.wait_ge(x_copied, fill(NT - 1, 4))
            turn_outputs(2 * NT - 2, 0)
            for part in range(4):
                multiply(PAIRS - 1, 3, part)
            pe.wait_ge(x_copied, fill(NT - 1, 5))
            turn_outputs(2 * NT - 1, 1)

        @block.scalar
        def _(act):
            def copy_queries(count, group, part):
                act.wait_ge(x_filled, count)
                nc.scalar.activation(q_turned[part][:, group * GROUP:(group + 1) * GROUP, :],
                                     ps_x[:, :].rearrange("p (h q) -> p h q", q=P), ACT.Copy).then_inc(x_copied, 1)

            def copy_outputs(count, g):
                act.wait_ge(x_filled, count)
                nc.scalar.activation(flat(o_parts[g]), ps_x[:, :], ACT.Copy).then_inc(x_copied, 1)

            def take_products(p, j, turned_before):
                cols = slice((j % 2) * 2 * P, (j % 2 + 1) * 2 * P)
                wait_for(act, x_filled, turned_before)
                act.wait_ge(multiplied, p + 1)
                nc.scalar.activation(o_turned[j // 2][:, cols], ps_o[:, cols], ACT.Copy).then_inc(o_copied, 1)

            def square(t):
                act.wait_ge(o_ready, 2 * t + 2)
                nc.scalar.activation(squares[:, :], o_att[:, :], ACT.Square,
                                     accum_out=att_squares[:, bass.ds(t, 1)]).then_inc(squared, 1)

            def exponentials(U, u, h):
                if h == 0:
                    act.wait_ge(max_ready, U + 1)
                    wait_for(act, turned, 4 * U - 12)
                nc.scalar.activation(probs[u % 4][:, h * L // 2:(h + 1) * L // 2], ps_s[h][:, :], ACT.Exp,
                                     bias=less_max[u % 2][:, :], scale=SCALE,
                                     accum_out=half_sums[u // GROUP][:, u % GROUP, h:h + 1]).then_inc(exp_done, 1)

            def round_hi(t, u, j):
                U = t * AH + u
                if j == 0 and u % 2 == 0:
                    wait_for(act, multiplied, 4 * t + u // 2 - 1)
                act.wait_ge(turned, 4 * U + j + 1)
                nc.scalar.activation(probs_hi[u // 2 % 2][:, 4 * j:4 * j + 4, u % 2, :],
                                     ps_t[j % 2][:, :].rearrange("p (c q) -> p c q", q=P), ACT.Copy).then_inc(hi_ready, 1)

            def body(t, first, last):
                for u in range(AH):
                    U = t * AH + u
                    more = not (last and u == AH - 1)
                    turning = not (first and u == 0)
                    if turning:
                        round_hi(t if u else t - 1, (u - 1) % AH, 0)
                    if u in (1, 2):
                        copy_queries(fill(t, u, first), 1, u - 1)
                    if u in (3, 4) and not first:
                        copy_outputs(fill(t, u), u - 3)
                    if u in (5, 6) and not last:
                        copy_queries(fill(t, u), 0, u - 5)
                    if u in (1, 3) and not first:
                        take_products(4 * t - 2 + u // 2, 2 + u // 2, fill(t - 1, 4))
                    if u in (5, 7):
                        take_products(4 * t + u // 2 - 2, u // 2 - 2, 0 if first else fill(t, 3))
                    if u == 6 and not first:
                        square(t - 1)
                    if turning:
                        round_hi(t if u else t - 1, (u - 1) % AH, 1)
                        round_hi(t if u else t - 1, (u - 1) % AH, 2)
                    if more:
                        exponentials(U + 1, (u + 1) % AH, 0)
                    if turning:
                        round_hi(t if u else t - 1, (u - 1) % AH, 3)
                    if more:
                        exponentials(U + 1, (u + 1) % AH, 1)

            for part in range(2):
                copy_queries(part + 1, 0, part)
            for h in range(2):
                exponentials(0, 0, h)
            tiles(act, body)
            for j in range(4):
                round_hi(NT - 1, AH - 1, j)
            take_products(4 * NT - 2, 2, fill(NT - 1, 4))
            copy_outputs(fill(NT - 1, 5), 0)
            take_products(4 * NT - 1, 3, fill(NT - 1, 4))
            copy_outputs(fill(NT - 1, 6), 1)
            square(NT - 1)

        @block.vector
        def _(dve):
            def half_maximum(U, s, h):
                dve.wait_ge(scored, 2 * U + h + 1)
                nc.vector.tensor_reduce(half_max[s][:, h:h + 1], ps_s[h][:, :], AX.X, ALU.max).then_inc(halved, 1)

            def maximum(U, s):
                dve.wait_ge(halved, 2 * U + 2)
                wait_for(dve, exp_done, 2 * U - 2)
                nc.vector.tensor_scalar(less_max[s][:, :], half_max[s][:, 0:1], half_max[s][:, 1:2], -SCALE,
                                        ALU.max, ALU.mult).then_inc(max_ready, 1)

            def remainder(U, u, j):
                dve.wait_ge(hi_ready, 4 * U + j + 1)
                hi, lo = (x[u // 2 % 2][:, 4 * j:4 * j + 4, u % 2, :] for x in (probs_hi, probs_lo))
                nc.vector.tensor_sub(lo, ps_t[j % 2][:, :].rearrange("p (c q) -> p c q", q=P), f32(hi)).then_inc(lo_ready, 1)

            def invert(t, g):
                n = 2 * t + g
                dve.wait_ge(exp_done, 2 * GROUP * (n + 1))
                nc.vector.tensor_reduce(sums[g][:, :], half_sums[g][:, :, :], AX.X, ALU.add).then_inc(summed, 1)
                wait_for(dve, o_ready, n - 1)
                dve.wait_ge(summed, n + 1)
                nc.vector.reciprocal(inverse[g][:, :], sums[g][:, :]).then_inc(inverted, 1)

            def body(t, first, last):
                for u in range(AH):
                    U, more = t * AH + u, not (last and u == AH - 1)
                    if u in (6, 7):
                        invert(t, u - 6)
                    if not (first and u < 2):
                        remainder(U - 2, (u - 2) % AH, 3)
                    if more:
                        half_maximum(U + 1, (u + 1) % 2, 0)
                    if not (first and u < 1):
                        remainder(U - 1, (u - 1) % AH, 0)
                    if more:
                        half_maximum(U + 1, (u + 1) % 2, 1)
                        maximum(U + 1, (u + 1) % 2)
                    if not (first and u < 1):
                        for j in (1, 2):
                            remainder(U - 1, (u - 1) % AH, j)

            dve.wait_ge(w_here, 16)
            prepare(dve, 0, 0)
            half_maximum(0, 0, 0)
            half_maximum(0, 0, 1)
            maximum(0, 0)
            tiles(dve, body)
            UNITS = AH * NT
            remainder(UNITS - 2, AH - 2, 3)
            for j in range(4):
                remainder(UNITS - 1, AH - 1, j)


def project_output(nc, const, o_squares, att_squares, x2_squares, hg_norm_w, att_norm_w, w_out, x, tok_scr, mix_scr,
                   x2_scr):
    ctx, sems = ExitStack(), []
    with ctx:
        def sb(name, shape, dt=FP32):
            return ctx.enter_context(nc.sbuf_tensor(name, shape, dt))

        def pair(name, shape, dt=FP32):
            return [sb(f"{name}{s}", shape, dt) for s in range(2)]

        def sem(name):
            return stage_semaphore(nc, sems, name)

        raw = [sb(f"w_out_raw{k}", [P, D]) for k in range(2)]
        w_hi, w_lo = sb("w_out_hi", [P, KD, D], F32R), sb("w_out_lo", [P, KD, D], F32R)
        hg_row, att_row = sb("hg_norm_row", [P, P]), sb("att_norm_row", [P, AQW])
        o_root, o_rstd = sb("o_root", [P, NT, HG]), sb("o_rstd", [P, NT, HG])
        a_root, a_rstd = sb("att_root", [P, NT]), sb("att_rstd", [P, NT])
        mix, gate, x_res = pair("mix", [P, D]), pair("gate", [P, HGW]), pair("x_res", [P, D])
        gain, scaled, normed = pair("gain", [P, HGW]), pair("hg_scaled", [P, HGW]), pair("mix_normed", [P, D])
        m_hi, m_lo = pair("mixT_hi", [P, KD, P], F32R), pair("mixT_lo", [P, KD, P], F32R)
        x2, squares = pair("x2", [P, D]), sb("x2_sq", [P, D])
        ps_t = [ctx.enter_context(nc.psum_tensor(f"mix_ps_t{j}", [P, BANK], FP32)) for j in range(2)]
        ps_o = [[ctx.enter_context(nc.psum_tensor(f"x2_ps{s}{j}", [P, BANK], FP32)) for j in range(2)] for s in range(2)]
        w_here = [sem(f"w_out_here{s}") for s in range(2)]
        rows_here, rooted, rstds = sem("norm_rows_here"), sem("roots_ready"), sem("rstds_ready")
        w_hi_ready, w_ready = sem("w_out_hi_ready"), sem("w_out_ready")
        mix_here, gate_here, x_here = ([sem(f"{n}_here{s}") for s in range(2)] for n in ("mix", "gate", "x_res"))
        gained, normed_ready = sem("gate_and_scale_ready"), sem("mix_normed_ready")
        turned, hi_ready, lo_ready = sem("mix_turned"), sem("mixT_hi_ready"), sem("mixT_lo_ready")
        done, added, squared = sem("x2_product_done"), sem("x2_ready"), sem("x2_squared")
        stored = [sem(f"x2_stored{s}") for s in range(2)]
        ident = const["ident"]
        block = stage_block(nc, ctx, sems)

        def heads(t):
            return t.rearrange("p (h c) -> p h c", c=P)

        def steps(eng, step):
            step(0, 0)
            step(1, 1)
            with eng.Fori(1, NT // 2) as i:
                step(2 * i, 0)
                step(2 * i + 1, 1)

        @block.sync
        def _(sp):
            sp.dma_start(hg_row[:, :], hg_norm_w.partition_broadcast(P)).then_inc(rows_here, 16)
            sp.dma_start(att_row[:, :], att_norm_w.partition_broadcast(P)).then_inc(rows_here, 16)

            def load(t, s):
                rows = bass.ds(t * P, P)
                wait_for(sp, gained, 2 * t - 2)
                sp.dma_start(gate[s][:, :], tok_scr[rows, C_G:C_G + HGW]).then_inc(gate_here[s], 16)
                wait_for(sp, normed_ready, 2 * t - 2)
                sp.dma_start(mix[s][:, :], mix_scr[rows, :]).then_inc(mix_here[s], 16)

            def load_x(t, s):
                rows = bass.ds(t * P, P)
                wait_for(sp, added, t - 1)
                sp.dma_start(x_res[s][:, :], x[rows, :]).then_inc(x_here[s], 16)

            def store(t, s):
                sp.wait_ge(added, t + 1)
                sp.dma_start(x2_scr[bass.ds(t * P, P), :], x2[s][:, :]).then_inc(stored[s], 16)

            load(0, 0)
            load(1, 1)
            for k in range(KD):
                if k >= 2:
                    sp.wait_ge(w_ready, k - 1)
                sp.dma_start(raw[k % 2][:, :], w_out[k * P:(k + 1) * P, :]).then_inc(w_here[k % 2], 16)
                if k == KD - 3:
                    load(2, 0)
            load_x(0, 0)
            load_x(1, 1)
            load(3, 1)
            for n in range(2):
                load_x(n + 2, n)
                store(n, n)
            with sp.Fori(2, NT // 2) as i:
                for s in range(2):
                    load(2 * i + s, s)
                    load_x(2 * i + s, s)
                    store(2 * i + s - 2, s)
            store(NT - 2, 0)
            store(NT - 1, 1)
            for s in range(2):
                sp.wait_ge(stored[s], 8 * NT)

        @block.gpsimd
        def _(pool):
            def step(t, s):
                pool.wait_ge(gate_here[s], 8 * (t - s) + 16)
                wait_for(pool, normed_ready, 2 * t - 2)
                nc.gpsimd.tensor_mul(heads(gain[s][:, :]), heads(gate[s][:, :]),
                                     hg_row[:, :].unsqueeze(1).to_broadcast([P, HG, P])).then_inc(gained, 1)
                pool.wait_ge(mix_here[s], 8 * (t - s) + 16)
                rstd = o_rstd[:, bass.ds(t, 1), :].rearrange("p o h -> p (o h)")
                nc.gpsimd.tensor_mul(heads(scaled[s][:, :]), heads(mix[s][:, 0:HGW]),
                                     rstd.unsqueeze(2).to_broadcast([P, HG, P])).then_inc(gained, 1)

            pool.wait_ge(rows_here, 32)
            pool.wait_ge(rstds, 2)
            steps(pool, step)

        @block.scalar
        def _(act):
            nc.scalar.activation(o_root[:, :, :], o_squares[:, :, :], ACT.Sqrt, bias=const["eps"][:, :],
                                 scale=1.0 / P).then_inc(rooted, 1)
            nc.scalar.activation(a_root[:, :], att_squares[:, :], ACT.Sqrt, bias=const["eps"][:, :],
                                 scale=1.0 / AQW).then_inc(rooted, 1)

            def round_hi(t, s):
                wait_for(act, done, t - 1)
                for j in range(2):
                    act.wait_ge(turned, 2 * t + j + 1)
                    nc.scalar.activation(m_hi[s][:, 4 * j:4 * j + 4, :], ps_t[j][:, :].rearrange("p (k t) -> p k t", t=P),
                                         ACT.Copy).then_inc(hi_ready, 1)

            def square(t, s):
                wait_for(act, squared, t)
                act.wait_ge(added, t + 1)
                nc.scalar.activation(squares[:, :], x2[s][:, :], ACT.Square,
                                     accum_out=x2_squares[:, bass.ds(t, 1)]).then_inc(squared, 1)

            round_hi(0, 0)
            round_hi(1, 1)
            for k in range(KD):
                act.wait_ge(w_here[k % 2], 16 * (k // 2) + 16)
                nc.scalar.activation(w_hi[:, k, :], raw[k % 2][:, :], ACT.Copy).then_inc(w_hi_ready, 1)
            def tiles(i):
                for s in range(2):
                    round_hi(2 * i + s, s)
                    square(2 * i + s - 2, s)

            tiles(1)
            with act.Fori(2, NT // 2) as i:
                tiles(i)
            square(NT - 2, 0)
            square(NT - 1, 1)

        @block.vector
        def _(dve):
            dve.wait_ge(rooted, 2)
            nc.vector.reciprocal(o_rstd[:, :, :], o_root[:, :, :]).then_inc(rstds, 1)
            nc.vector.reciprocal(a_rstd[:, :], a_root[:, :]).then_inc(rstds, 1)

            def normalise(t, s):
                dve.wait_ge(mix_here[s], 8 * (t - s) + 16)
                wait_for(dve, turned, 2 * t - 2)
                nc.vector.scalar_tensor_tensor(out=normed[s][:, HGW:D], in0=mix[s][:, HGW:D],
                                               scalar=a_rstd[:, bass.ds(t, 1)], in1=att_row[:, :],
                                               op0=ALU.mult, op1=ALU.mult).then_inc(normed_ready, 1)
                dve.wait_ge(gained, 2 * t + 2)
                nc.vector.tensor_mul(normed[s][:, 0:HGW], gain[s][:, :], scaled[s][:, :]).then_inc(normed_ready, 1)

            def remainder(t, s):
                for j in range(2):
                    dve.wait_ge(hi_ready, 2 * t + j + 1)
                    nc.vector.tensor_sub(m_lo[s][:, 4 * j:4 * j + 4, :], ps_t[j][:, :].rearrange("p (k t) -> p k t", t=P),
                                         f32(m_hi[s][:, 4 * j:4 * j + 4, :])).then_inc(lo_ready, 1)

            def add(t, s):
                dve.wait_ge(done, t + 1)
                dve.wait_ge(x_here[s], 8 * (t - s) + 16)
                wait_for(dve, stored[s], 8 * (t - s))
                wait_for(dve, squared, t - 1)
                nc.vector.tensor_add(x2[s][:, 0:BANK], ps_o[s][0][:, :], x_res[s][:, 0:BANK])
                nc.vector.tensor_add(x2[s][:, BANK:D], ps_o[s][1][:, :], x_res[s][:, BANK:D]).then_inc(added, 1)

            dve.wait_ge(rows_here, 32)
            dve.wait_ge(rstds, 2)
            normalise(0, 0)
            normalise(1, 1)
            remainder(0, 0)
            remainder(1, 1)
            for k in range(KD):
                if k == KD - 1:
                    normalise(2, 0)
                dve.wait_ge(w_hi_ready, k + 1)
                nc.vector.tensor_sub(w_lo[:, k, :], raw[k % 2][:, :], f32(w_hi[:, k, :])).then_inc(w_ready, 1)
            def tiles(i):
                for s in range(2):
                    normalise(2 * i + s, s)
                    add(2 * i + s - 2, s)
                    remainder(2 * i + s, s)

            add(0, 0)
            remainder(2, 0)
            normalise(3, 1)
            add(1, 1)
            remainder(3, 1)
            with dve.Fori(2, NT // 2) as i:
                tiles(i)
            add(NT - 2, 0)
            add(NT - 1, 1)

        @block.tensor
        def _(pe):
            def turn(t, s):
                pe.wait_ge(normed_ready, 2 * t + 2)
                for j in range(2):
                    wait_for(pe, lo_ready, 2 * t + j - 1)
                    for k in range(4 * j, 4 * j + 4):
                        last = nc.tensor.transpose(ps_t[j][:, (k % 4) * P:(k % 4 + 1) * P],
                                                   normed[s][:, k * P:(k + 1) * P], ident[:, :])
                    last.then_inc(turned, 1)

            def multiply(t, s):
                pe.wait_ge(lo_ready, 2 * t + 2)
                wait_for(pe, added, t - 1)
                for j in range(2):
                    cols = slice(j * BANK, (j + 1) * BANK)
                    last = split_products(nc, ps_o[s][j][:, :], (lambda k: m_hi[s][:, k, :], lambda k: m_lo[s][:, k, :]),
                                          (lambda k: w_hi[:, k, cols], lambda k: w_lo[:, k, cols]), KD)
                last.then_inc(done, 1)

            turn(0, 0)
            turn(1, 1)
            pe.wait_ge(lo_ready, 4)
            for k0 in range(KD):
                if k0 == KD - 1:
                    turn(2, 0)
                pe.wait_ge(w_ready, k0 + 1)
                for s in range(2):
                    for j in range(2):
                        cols = slice(j * BANK, (j + 1) * BANK)
                        last = split_products(nc, ps_o[s][j][:, :], (lambda k: m_hi[s][:, k, :], lambda k: m_lo[s][:, k, :]),
                                              (lambda k: w_hi[:, k, cols], lambda k: w_lo[:, k, cols]), KD, [k0])
                    if k0 == KD - 1:
                        last.then_inc(done, 1)

            def tiles(i):
                turn(2 * i, 0)
                multiply(2 * i - 1, 1)
                turn(2 * i + 1, 1)
                multiply(2 * i, 0)

            turn(3, 1)
            multiply(2, 0)
            with pe.Fori(2, NT // 2) as i:
                tiles(i)
            multiply(NT - 1, 1)


def feed_forward(nc, const, half, x2_squares, w2_row, final_row, w_gate_up, w_down, x2_scr, out):
    NP = NF // 2
    TB = HALF // BANK
    YB = HT * D // BANK
    ctx, sems = ExitStack(), []
    with ctx:
        def sb(name, shape, dt=FP32):
            return ctx.enter_context(nc.sbuf_tensor(f"{name}_{half}", shape, dt))

        def pair(name, shape, dt=FP32):
            return [sb(f"{name}{s}", shape, dt) for s in range(2)]

        def pb(name, n):
            return [ctx.enter_context(nc.psum_tensor(f"{name}{j}_{half}", [P, BANK], FP32)) for j in range(n)]

        def sem(name):
            return stage_semaphore(nc, sems, f"{name}_{half}")

        y = sb("y", [P, HT, D])
        hT_hi, hT_lo = sb("h2T_hi", [P, KD, HALF], F32R), sb("h2T_lo", [P, KD, HALF], F32R)
        gu_raw, gu_hi, gu_lo = pair("gu_raw", [P, KD, 2, P]), pair("gu_hi", [P, KD, 2, P], F32R), pair("gu_lo", [P, KD, 2, P], F32R)
        d_raw, d_hi, d_lo = sb("d_raw", [P, 2, D]), sb("d_hi", [P, 2, D], F32R), sb("d_lo", [P, 2, D], F32R)
        silu, act_f = pair("silu", [P, BANK]), sb("act", [P, max(HALF, D)])
        act_hi, act_lo = pair("act_hi", [P, HALF], F32R), pair("act_lo", [P, HALF], F32R)
        h2 = [sb("h2", [P, D]), act_f]
        root, rstd = sb("x2_root", [P, HT]), sb("x2_rstd", [P, HT])
        y_total, y_root, y_rstd = sb("y_total", [P, HT]), sb("y_root", [P, HT]), sb("y_rstd", [P, HT])
        ps_g, ps_u, ps_y = pb("ps_g", TB), pb("ps_u", TB), pb("ps_y", 4)
        y_here, rooted, rstds = [sem(f"y_here{t}") for t in range(HT)], sem("x2_root_ready"), sem("x2_rstd_ready")
        h2_ready, turned, hi_ready, lo_ready = sem("h2_ready"), sem("h2_turned"), sem("h2T_hi_ready"), sem("h2T_lo_ready")
        gu_here, d_here = [sem(f"gu_here{s}") for s in range(2)], sem("d_here")
        gu_rounded, gu_ready, d_rounded, d_ready = sem("gu_hi_ready"), sem("gu_ready"), sem("d_hi_ready"), sem("d_ready")
        gated, silued, activated = sem("gate_up_done"), sem("silu_ready"), sem("act_ready")
        act_rounded, act_ready = sem("act_hi_ready"), sem("act_split")
        down_done, y_added = sem("down_done"), sem("y_added")
        y_squared, y_rooted, y_scale, out_ready = sem("y_squared"), sem("y_root_ready"), sem("y_rstd_ready"), sem("out_ready")
        stored = sem("out_stored")
        tile0 = half * HT
        gu_cols = w_gate_up.rearrange("(k p) (a n) -> a p k n", p=P, a=2)
        d_rows = w_down.rearrange("(i a p) n -> i p a n", p=P, a=2)
        block = stage_block(nc, ctx, sems)

        @block.sync
        def _(sp):
            def load_gate_up(f, s):
                wait_for(sp, gu_ready, f - 1)
                for a in range(2):
                    sp.dma_start(gu_raw[s][:, :, a, :], gu_cols[a, :, :, bass.ds(f * P, P)]).then_inc(gu_here[s], 16)

            def load_down(i):
                wait_for(sp, d_ready, i)
                sp.dma_start(d_raw[:, :, :], d_rows[bass.ds(i, 1), :, :, :].rearrange("o p a n -> (o p) a n")).then_inc(d_here, 16)

            for t in range(HT):
                sp.dma_start(y[:, t, :], x2_scr[(tile0 + t) * P:(tile0 + t + 1) * P, :]).then_inc(y_here[t], 16)
                if t == 1:
                    load_gate_up(0, 0)
            load_gate_up(1, 1)
            load_down(0)
            with sp.Fori(1, NP) as i:
                load_gate_up(2 * i, 0)
                load_gate_up(2 * i + 1, 1)
                load_down(i)
            for t in range(HT):
                sp.wait_ge(out_ready, t + 1)
                sp.dma_start(out[(tile0 + t) * P:(tile0 + t + 1) * P, :], y[:, t, :]).then_inc(stored, 16)
            sp.wait_ge(stored, 16 * HT)

        @block.gpsimd
        def _(pool):
            def split_gate_up(f, s):
                pool.wait_ge(gu_rounded, f + 1)
                nc.gpsimd.tensor_sub(gu_lo[s][:, :, :, :], gu_raw[s][:, :, :, :], f32(gu_hi[s][:, :, :, :])).then_inc(gu_ready, 1)

            def split_down(i):
                pool.wait_ge(d_rounded, i + 1)
                nc.gpsimd.tensor_sub(d_lo[:, :, :], d_raw[:, :, :], f32(d_hi[:, :, :])).then_inc(d_ready, 1)

            split_gate_up(0, 0)
            split_gate_up(1, 1)
            with pool.Fori(0, NP - 1) as i:
                split_gate_up(2 * i + 2, 0)
                split_down(i)
                split_gate_up(2 * i + 3, 1)
            split_down(NP - 1)

        @block.scalar
        def _(act):
            def round_gate_up(f, s):
                act.wait_ge(gu_here[s], 16 * (f - s) + 32)
                wait_for(act, gated, 2 * TB * (f - 1))
                nc.scalar.activation(gu_hi[s][:, :, :, :], gu_raw[s][:, :, :, :], ACT.Copy).then_inc(gu_rounded, 1)

            def round_down(i):
                act.wait_ge(d_here, 16 * i + 16)
                wait_for(act, down_done, YB * i)
                nc.scalar.activation(d_hi[:, :, :], d_raw[:, :, :], ACT.Copy).then_inc(d_rounded, 1)

            def silus(f):
                for tb in range(TB):
                    act.wait_ge(gated, 2 * TB * f + 2 * tb + 1)
                    wait_for(act, activated, TB * f + tb - 1)
                    nc.scalar.activation(silu[tb][:, :], ps_g[tb][:, :], ACT.Silu).then_inc(silued, 1)

            def round_act(f, s, i):
                wait_for(act, down_done, YB * i)
                for tb in range(TB):
                    cols = slice(tb * BANK, (tb + 1) * BANK)
                    act.wait_ge(activated, TB * f + tb + 1)
                    nc.scalar.activation(act_hi[s][:, cols], act_f[:, cols], ACT.Copy).then_inc(act_rounded, 1)

            nc.scalar.activation(root[:, :], x2_squares[:, tile0:tile0 + HT], ACT.Sqrt, bias=const["eps"][:, :],
                                 scale=1.0 / D).then_inc(rooted, 1)
            for t in range(HT):
                if t in (2, 6):
                    round_gate_up(t // 4, t // 4)
                for j in range(2):
                    act.wait_ge(turned, 2 * t + j + 1)
                    nc.scalar.activation(hT_hi[:, 4 * j:4 * j + 4, t * P:(t + 1) * P],
                                         ps_y[2 * (t % 2) + j][:, :].rearrange("p (k t) -> p k t", t=P),
                                         ACT.Copy).then_inc(hi_ready, 1)

            def body(i, more):
                silus(2 * i)
                if more:
                    round_gate_up(2 * i + 2, 0)
                round_act(2 * i, 0, i)
                round_down(i)
                silus(2 * i + 1)
                round_act(2 * i + 1, 1, i)
                if more:
                    round_gate_up(2 * i + 3, 1)

            body(0, True)
            with act.Fori(1, NP - 1) as i:
                body(i, True)
            body(NP - 1, False)
            for t in range(HT):
                wait_for(act, y_squared, t - 1)
                act.wait_ge(y_added, YB * (NP - 1) + 2 * t + 2)
                nc.scalar.activation(h2[t % 2][:, :], y[:, t, :], ACT.Square, accum_out=y_total[:, t:t + 1]).then_inc(y_squared, 1)
                act.wait_ge(y_squared, t + 1)
                nc.scalar.activation(y_root[:, t:t + 1], y_total[:, t:t + 1], ACT.Sqrt, bias=const["eps"][:, :],
                                     scale=1.0 / D).then_inc(y_rooted, 1)

        @block.vector
        def _(dve):
            dve.wait_ge(rooted, 1)
            nc.vector.reciprocal(rstd[:, :], root[:, :]).then_inc(rstds, 1)
            dve.wait_ge(rstds, 1)
            for t in range(HT + 1):
                if t < HT:
                    dve.wait_ge(y_here[t], 16)
                    if t >= 2:
                        dve.wait_ge(turned, 2 * t - 2)
                    nc.vector.scalar_tensor_tensor(out=h2[t % 2][:, :], in0=y[:, t, :], scalar=rstd[:, t:t + 1],
                                                   in1=w2_row[:, :], op0=ALU.mult, op1=ALU.mult).then_inc(h2_ready, 1)
                if t >= 1:
                    for j in range(2):
                        cols = (slice(None), slice(4 * j, 4 * j + 4), slice((t - 1) * P, t * P))
                        dve.wait_ge(hi_ready, 2 * t - 1 + j)
                        nc.vector.tensor_sub(hT_lo[cols], ps_y[2 * ((t - 1) % 2) + j][:, :].rearrange("p (k t) -> p k t", t=P),
                                             f32(hT_hi[cols])).then_inc(lo_ready, 1)

            def activate(f):
                for tb in range(TB):
                    dve.wait_ge(silued, TB * f + tb + 1)
                    dve.wait_ge(gated, 2 * TB * f + 2 * tb + 2)
                    wait_for(dve, act_rounded, TB * (f - 1) + tb + 1)
                    wait_for(dve, act_ready, TB * (f - 1) + tb + 1)
                    nc.vector.tensor_mul(act_f[:, tb * BANK:(tb + 1) * BANK], silu[tb][:, :], ps_u[tb][:, :]).then_inc(activated, 1)

            def remainder(f, s):
                for tb in range(TB):
                    cols = slice(tb * BANK, (tb + 1) * BANK)
                    dve.wait_ge(act_rounded, TB * f + tb + 1)
                    nc.vector.tensor_sub(act_lo[s][:, cols], act_f[:, cols], f32(act_hi[s][:, cols])).then_inc(act_ready, 1)

            def add(i, banks=range(YB)):
                for n in banks:
                    t, cols = n // 2, slice((n % 2) * BANK, (n % 2 + 1) * BANK)
                    dve.wait_ge(down_done, YB * i + n + 1)
                    wait_for(dve, y_added, YB * (i - 1) + n + 1)
                    nc.vector.tensor_add(y[:, t, cols], ps_y[n % 4][:, :], y[:, t, cols]).then_inc(y_added, 1)

            def body(i, first):
                activate(2 * i)
                if not first:
                    add(i - 1)
                remainder(2 * i, 0)
                activate(2 * i + 1)
                remainder(2 * i + 1, 1)

            body(0, True)
            body(1, False)
            with dve.Fori(2, NP) as i:
                body(i, False)
            for t in range(HT + 1):
                if t < HT:
                    add(NP - 1, (2 * t, 2 * t + 1))
                if t >= 1:
                    one = slice(t - 1, t)
                    dve.wait_ge(y_rooted, t)
                    nc.vector.reciprocal(y_rstd[:, one], y_root[:, one]).then_inc(y_scale, 1)
                    dve.wait_ge(y_scale, t)
                    nc.vector.scalar_tensor_tensor(out=y[:, t - 1, :], in0=y[:, t - 1, :], scalar=y_rstd[:, one],
                                                   in1=final_row[:, :], op0=ALU.mult, op1=ALU.mult).then_inc(out_ready, 1)

        @block.tensor
        def _(pe):
            def turn(t):
                pe.wait_ge(h2_ready, t + 1)
                for j in range(2):
                    if t >= 2:
                        pe.wait_ge(lo_ready, 2 * t + j - 3)
                    for k in range(4 * j, 4 * j + 4):
                        last = nc.tensor.transpose(ps_y[2 * (t % 2) + j][:, (k % 4) * P:(k % 4 + 1) * P],
                                                   h2[t % 2][:, k * P:(k + 1) * P], const["ident"][:, :])
                    last.then_inc(turned, 1)

            def gate_up(f, s):
                pe.wait_ge(gu_ready, f + 1)
                for tb in range(TB):
                    cols = slice(tb * BANK, (tb + 1) * BANK)
                    for a, ps in ((0, ps_g), (1, ps_u)):
                        wait_for(pe, activated, TB * (f - 1) + tb + 1)
                        split_products(nc, ps[tb][:, :], (lambda k: gu_hi[s][:, k, a, :], lambda k: gu_lo[s][:, k, a, :]),
                                       (lambda k: hT_hi[:, k, cols], lambda k: hT_lo[:, k, cols]), KD).then_inc(gated, 1)

            def down(i):
                pe.wait_ge(d_ready, i + 1)
                pe.wait_ge(act_ready, 2 * TB * (i + 1))
                for n in range(YB):
                    t, cols = n // 2, slice((n % 2) * BANK, (n % 2 + 1) * BANK)
                    toks = slice(t * P, (t + 1) * P)
                    wait_for(pe, y_added, YB * i + n - 3)
                    split_products(nc, ps_y[n % 4][:, :], (lambda a: act_hi[a][:, toks], lambda a: act_lo[a][:, toks]),
                                   (lambda a: d_hi[:, a, cols], lambda a: d_lo[:, a, cols]), 2).then_inc(down_done, 1)

            def pair_of_tiles(i):
                gate_up(2 * i, 0)
                down(i - 1)
                gate_up(2 * i + 1, 1)

            for t in range(HT // 2):
                turn(t)
            pe.wait_ge(gu_ready, 1)
            for tb in range(TB):
                pe.wait_ge(lo_ready, HT * (tb + 1))
                cols = slice(tb * BANK, (tb + 1) * BANK)
                for a, ps in ((0, ps_g), (1, ps_u)):
                    for part in range(2):
                        last = split_products(nc, ps[tb][:, :],
                                              (lambda k: gu_hi[0][:, k, a, :], lambda k: gu_lo[0][:, k, a, :]),
                                              (lambda k: hT_hi[:, k, cols], lambda k: hT_lo[:, k, cols]), KD,
                                              range(part * KD // 2, (part + 1) * KD // 2))
                        if part == 1:
                            last.then_inc(gated, 1)
                        if tb == 0:
                            turn(HT // 2 + 2 * a + part)
            gate_up(1, 1)
            pair_of_tiles(1)
            with pe.Fori(2, NP) as i:
                pair_of_tiles(i)
            down(NP - 1)


def load_rows(nc, rows):
    ctx, sems = ExitStack(), []
    with ctx:
        rows_here = stage_semaphore(nc, sems, "final_rows_here")
        block = stage_block(nc, ctx, sems)

        @block.sync
        def _(sp):
            for tile, weights in rows:
                sp.dma_start(tile[:, :], weights.partition_broadcast(P)).then_inc(rows_here, 16)
            sp.wait_ge(rows_here, 16 * len(rows))


def encoder_layer(nc, out, x, norm1_w, w_in, lb_logits, hg_norm_w, q_norm_w, k_norm_w, att_norm_w, w_out, norm2_w,
                  w_gate_up, w_down, final_norm_w, rope):
    ctx = ExitStack()
    with ctx:
        def sb(name, shape, dt=FP32):
            return ctx.enter_context(nc.sbuf_tensor(name, shape, dt))

        def scratch(name, shape):
            return nc.dram_tensor(name, shape, FP32, kind="Internal").ap()

        q_scr, f_scr, k_scr = scratch("q_scr", (HG, P, L)), scratch("f_scr", (2 * HG, P, L)), scratch("k_scr", (2 * HG, P, L))
        tok_scr, mix_scr, x2_scr = scratch("tok_scr", (L, TOKEN_COLS)), scratch("mix_scr", (L, D)), scratch("x2_scr", (L, D))
        const = {"ident": sb("ident", [P, P]), "eps": sb("eps", [P, 1])}
        head_squares, head_rstd = sb("head_squares", [P, NT, NS]), sb("head_rstd", [P, NT, NS])
        o_squares, att_squares, x2_squares = sb("o_squares", [P, NT, HG]), sb("att_squares", [P, NT]), sb("x2_squares", [P, NT])
        with nc.sbuf_tensor("hT_hi", [P, KD, L], F32R) as hT_hi, nc.sbuf_tensor("hT_lo", [P, KD, L], F32R) as hT_lo:
            project_input(nc, const, head_squares, hT_hi, hT_lo, x[0], norm1_w[0], w_in[0], lb_logits, q_scr, f_scr,
                          k_scr, tok_scr)
        with nc.sbuf_tensor("o_back", [P, NT, HGW], FP32) as o_back:
            for forward in (False, True):
                recurrence(nc, const, forward, o_back, o_squares, q_scr, f_scr, k_scr, tok_scr, mix_scr)
        with nc.sbuf_tensor("k_turned", [P, KVH, L], F32R) as k_turned, \
                nc.sbuf_tensor("v_split", [P, NT, KVH, 2 * DH], F32R) as v_split, \
                nc.sbuf_tensor("rope_sb", [P, 2, NT, DH // 2], FP32) as rope_sb:
            prepare_keys(nc, const, head_squares, head_rstd, rope_sb, k_turned, v_split, k_norm_w[0], rope, tok_scr)
            attention(nc, const, head_rstd, rope_sb, k_turned, v_split, att_squares, q_norm_w[0], tok_scr, mix_scr)
        project_output(nc, const, o_squares, att_squares, x2_squares, hg_norm_w[0], att_norm_w[0], w_out[0], x[0],
                       tok_scr, mix_scr, x2_scr)
        w2_row, final_row = sb("norm2_row", [P, D]), sb("final_row", [P, D])
        load_rows(nc, [(w2_row, norm2_w[0]), (final_row, final_norm_w)])
        for half in range(2):
            feed_forward(nc, const, half, x2_squares, w2_row, final_row, w_gate_up[0], w_down[0], x2_scr, out[0])


_INS = ["x", "norm1_w", "w_in", "lb_logits", "hg_norm_w", "q_norm_w", "k_norm_w", "att_norm_w", "w_out", "norm2_w",
        "w_gate_up", "w_down", "final_norm_w"]


def kernel(**inputs):
    import numpy as _np
    import concourse.bacc as _bacc
    from concourse import mybir as _mybir
    from concourse.bass_utils import run_bass_kernel_spmd as _run

    nc = _bacc.Bacc("TRN2", target_bir_lowering=False, num_devices=1)
    arrays = {f"in_{n}_dram": _np.ascontiguousarray(inputs[n]) for n in _INS}
    grid_w, pairs = 64, 32
    freqs = _np.float32(10000.0) ** (-_np.arange(0, 32, 2, dtype=_np.float32) / _np.float32(32))
    token = _np.arange(2048)
    angle = _np.concatenate([(token // grid_w).astype(_np.float32)[:, None] * freqs,
                             (token % grid_w).astype(_np.float32)[:, None] * freqs], axis=-1).astype(_np.float32)
    arrays["in_rope_dram"] = _np.stack([_np.cos(angle), _np.sin(angle)]).astype(_np.float32).reshape(2, 2048, pairs)
    args = {}
    for name in _INS + ["rope"]:
        a = arrays[f"in_{name}_dram"]
        args[name] = nc.dram_tensor(f"in_{name}_dram", a.shape, _mybir.dt.from_np(a.dtype), kind="ExternalInput").ap()
    out = nc.dram_tensor("out_0_dram", (1, 2048, 1024), _mybir.dt.float32, kind="ExternalOutput").ap()
    encoder_layer(nc, out=out, **args)
    r = _run(nc, [arrays], core_ids=[0])
    return r.results[0]["out_0_dram"]
```
